# Optimizing a Trainium2 kernel written in Bass

```python
import jax, jax.numpy as jnp
from jax import lax
import numpy as np

D_MODEL = 1024
BATCH = 1
SEQ = 2048
DEPTH = 1

CHUNK = 64
RET_HEADS = 4
RET_DK = 128
RET_DV = 128
GDN_HEADS = 4
GDN_DK = 128
GDN_DV = 128
CONV_WIDTH = 4
D_FF = 4 * D_MODEL
ROPE_BASE = 10000.0
NORM_EPS = 1e-6
RET_QK_W = RET_HEADS * RET_DK
RET_W = RET_HEADS * RET_DV
GDN_QK_W = GDN_HEADS * GDN_DK
GDN_W = GDN_HEADS * GDN_DV
MIX_W = RET_W + GDN_W
CONV_CH = 2 * GDN_QK_W + GDN_W
D_IN = 2 * RET_QK_W + 2 * RET_W + 2 * GDN_QK_W + 2 * GDN_W + 2 * GDN_HEADS
N_MOD = 6

kernel_name = "hybrid_retention_gdn_adaln_block"

def rmsnorm(x, w):
    xf = x.astype(jnp.float32)
    y = xf * lax.rsqrt(jnp.mean(xf * xf, axis=-1, keepdims=True) + NORM_EPS)
    return (y * w.astype(jnp.float32)).astype(x.dtype)

def modulate(h, shift, scale):
    return h * (1.0 + scale[:, None, :]) + shift[:, None, :]

def l2norm(x):
    return x * lax.rsqrt(jnp.sum(x * x, axis=-1, keepdims=True) + NORM_EPS)

def rotary(x, positions):
    d = x.shape[-1]
    inv = ROPE_BASE ** (-jnp.arange(0, d, 2, dtype=jnp.float32) / d)
    ang = positions[:, None] * inv[None, :]
    cos = jnp.cos(ang)[None, :, None, :]
    sin = jnp.sin(ang)[None, :, None, :]
    x1, x2 = jnp.split(x, 2, axis=-1)
    return jnp.concatenate([x1 * cos - x2 * sin, x1 * sin + x2 * cos], axis=-1)

def causal_depthwise_conv(x, w):
    ch = x.shape[-1]
    return lax.conv_general_dilated(
        x, w[:, None, :], window_strides=(1,), padding=[(CONV_WIDTH - 1, 0)],
        dimension_numbers=("NWC", "WIO", "NWC"), feature_group_count=ch)

def to_chunks(x):
    b, t, h, d = x.shape
    return x.reshape(b, t // CHUNK, CHUNK, h, d).transpose(0, 3, 1, 2, 4)

def from_chunks(x):
    b, h, n, c, d = x.shape
    return x.transpose(0, 2, 3, 1, 4).reshape(b, n * c, h, d)

def retention_chunkwise(q, k, v):
    n_heads = q.shape[1]
    log_gamma = jnp.log(1.0 - 2.0 ** (-5.0 - jnp.arange(n_heads, dtype=jnp.float32)))
    j = jnp.arange(CHUNK, dtype=jnp.float32)
    intra_decay = jnp.exp(log_gamma[:, None, None] * jnp.abs(j[:, None] - j[None, :]))
    scores = jnp.einsum("bhncd,bhnsd->bhncs", q, k) * intra_decay[None, :, None]
    o_intra = jnp.einsum("bhncs,bhnsv->bhncv", scores, v)
    q_dec = q * jnp.exp(log_gamma[:, None] * (j + 1.0)[None, :])[None, :, None, :, None]
    k_dec = k * jnp.exp(log_gamma[:, None] * (CHUNK - 1.0 - j)[None, :])[None, :, None, :, None]
    chunk_decay = jnp.exp(log_gamma * CHUNK)[None, :, None, None]

    def step(state, xs):
        qd, kd, vc = xs
        o = jnp.einsum("bhcd,bhdv->bhcv", qd, state)
        state = state * chunk_decay + jnp.einsum("bhcd,bhcv->bhdv", kd, vc)
        return state, o

    b, h, _, _, dk = q.shape
    s0 = jnp.zeros((b, h, dk, v.shape[-1]), jnp.float32)
    xs = (jnp.moveaxis(q_dec, 2, 0), jnp.moveaxis(k_dec, 2, 0), jnp.moveaxis(v, 2, 0))
    _, o_cross = lax.scan(step, s0, xs)
    return o_intra + jnp.moveaxis(o_cross, 0, 2)

def gated_delta_rule_chunked(q, k, v, g, beta):
    gc = jnp.cumsum(g, axis=-1)
    idx = jnp.arange(CHUNK)
    tril = idx[:, None] >= idx[None, :]
    strict = idx[:, None] > idx[None, :]
    diff = gc[..., :, None] - gc[..., None, :]
    decay = jnp.exp(jnp.where(tril, diff, -jnp.inf))
    kk = jnp.einsum("bhncd,bhnsd->bhncs", k, k)
    lower = jnp.where(strict, beta[..., :, None] * kk * decay, 0.0)
    eye = jnp.eye(CHUNK, dtype=jnp.float32)
    rhs = jnp.concatenate([beta[..., None] * v, beta[..., None] * k * jnp.exp(gc)[..., None]], axis=-1)
    a_mat = jnp.broadcast_to(eye, lower.shape) + lower
    sol = lax.linalg.triangular_solve(a_mat, rhs, left_side=True, lower=True, unit_diagonal=True)
    dv = v.shape[-1]
    u, w = sol[..., :dv], sol[..., dv:]
    attn = jnp.einsum("bhncd,bhnsd->bhncs", q, k) * decay
    q_g = q * jnp.exp(gc)[..., None]
    g_last = gc[..., -1]
    k_dec = k * jnp.exp(g_last[..., None] - gc)[..., None]

    def step(state, xs):
        qg, at, uc, wc, kd, gl = xs
        v_new = uc - jnp.einsum("bhcd,bhdv->bhcv", wc, state)
        o = jnp.einsum("bhcd,bhdv->bhcv", qg, state) + jnp.einsum("bhcs,bhsv->bhcv", at, v_new)
        state = state * jnp.exp(gl)[:, :, None, None] + jnp.einsum("bhcd,bhcv->bhdv", kd, v_new)
        return state, o

    b, h, _, _, dk = q.shape
    s0 = jnp.zeros((b, h, dk, dv), jnp.float32)
    xs = tuple(jnp.moveaxis(t, 2, 0) for t in (q_g, attn, u, w, k_dec, g_last))
    _, o = lax.scan(step, s0, xs)
    return jnp.moveaxis(o, 0, 2)

def token_mix(proj, positions, conv_w, a_log, dt_bias, ret_norm_w, gdn_norm_w):
    b, t, _ = proj.shape
    sizes = (RET_QK_W, RET_QK_W, RET_W, RET_W, GDN_QK_W, GDN_QK_W, GDN_W, GDN_W, GDN_HEADS, GDN_HEADS)
    cuts = np.cumsum(sizes)[:-1].tolist()
    rq, rk, rv, rg, gq, gk, gv, gz, ga, gb = jnp.split(proj, cuts, axis=-1)

    rq = rotary(rq.reshape(b, t, RET_HEADS, RET_DK), positions)
    rk = rotary(rk.reshape(b, t, RET_HEADS, RET_DK), positions) * (RET_DK ** -0.5)
    rv = rv.reshape(b, t, RET_HEADS, RET_DV)
    ro = from_chunks(retention_chunkwise(to_chunks(rq), to_chunks(rk), to_chunks(rv)))
    mu = jnp.mean(ro, axis=-1, keepdims=True)
    var = jnp.mean(jnp.square(ro - mu), axis=-1, keepdims=True)
    ro = ((ro - mu) * lax.rsqrt(var + NORM_EPS)).reshape(b, t, RET_W) * ret_norm_w
    ret_out = ro * jax.nn.silu(rg)

    qkv = jax.nn.silu(causal_depthwise_conv(jnp.concatenate([gq, gk, gv], axis=-1), conv_w))
    gq, gk, gv = jnp.split(qkv, [GDN_QK_W, 2 * GDN_QK_W], axis=-1)
    gq = l2norm(gq.reshape(b, t, GDN_HEADS, GDN_DK)) * (GDN_DK ** -0.5)
    gk = l2norm(gk.reshape(b, t, GDN_HEADS, GDN_DK))
    gv = gv.reshape(b, t, GDN_HEADS, GDN_DV)
    beta = jax.nn.sigmoid(gb)
    g = -jnp.exp(a_log) * jax.nn.softplus(ga + dt_bias)
    n = t // CHUNK
    g_c = g.reshape(b, n, CHUNK, GDN_HEADS).transpose(0, 3, 1, 2)
    beta_c = beta.reshape(b, n, CHUNK, GDN_HEADS).transpose(0, 3, 1, 2)
    go = from_chunks(gated_delta_rule_chunked(to_chunks(gq), to_chunks(gk), to_chunks(gv), g_c, beta_c))
    go = go * lax.rsqrt(jnp.mean(go * go, axis=-1, keepdims=True) + NORM_EPS) * gdn_norm_w
    gdn_out = go.reshape(b, t, GDN_W) * jax.nn.silu(gz)

    return jnp.concatenate([ret_out, gdn_out], axis=-1)

def setup_inputs(seed: int = 0) -> dict:
    key = jax.random.key(seed)
    ks = jax.random.split(key, 20)
    f32 = jnp.float32
    nrm = lambda k, shape, s: jax.random.normal(k, shape, f32) * s
    dt = jnp.exp(jax.random.uniform(ks[7], (DEPTH, GDN_HEADS), f32, np.log(1e-3), np.log(1e-1)))
    return {
        "x": nrm(ks[0], (BATCH, SEQ, D_MODEL), 1.0),
        "c": nrm(ks[1], (BATCH, D_MODEL), 1.0),
        "ada_w": nrm(ks[2], (DEPTH, D_MODEL, N_MOD * D_MODEL), 0.5 * D_MODEL ** -0.5),
        "ada_b": nrm(ks[3], (DEPTH, N_MOD * D_MODEL), 0.02),
        "norm_mix_w": 1.0 + nrm(ks[4], (DEPTH, D_MODEL), 0.02),
        "w_in": nrm(ks[5], (DEPTH, D_MODEL, D_IN), D_MODEL ** -0.5),
        "conv_w": nrm(ks[6], (DEPTH, CONV_WIDTH, CONV_CH), CONV_WIDTH ** -0.5),
        "a_log": jnp.log(jax.random.uniform(ks[8], (DEPTH, GDN_HEADS), f32, 1.0, 16.0)),
        "dt_bias": dt + jnp.log(-jnp.expm1(-dt)),
        "ret_norm_w": 1.0 + nrm(ks[9], (DEPTH, RET_W), 0.02),
        "gdn_norm_w": 1.0 + nrm(ks[10], (DEPTH, GDN_DV), 0.02),
        "w_out": nrm(ks[11], (DEPTH, MIX_W, D_MODEL), MIX_W ** -0.5),
        "norm_mlp_w": 1.0 + nrm(ks[12], (DEPTH, D_MODEL), 0.02),
        "w_ff1": nrm(ks[13], (DEPTH, D_MODEL, D_FF), D_MODEL ** -0.5),
        "w_ff2": nrm(ks[14], (DEPTH, D_FF, D_MODEL), D_FF ** -0.5),
        "norm_final_w": 1.0 + nrm(ks[15], (D_MODEL,), 0.02),
    }

def reference(x, c, ada_w, ada_b, norm_mix_w, w_in, conv_w, a_log, dt_bias, ret_norm_w,
              gdn_norm_w, w_out, norm_mlp_w, w_ff1, w_ff2, norm_final_w):
    t = x.shape[1]
    positions = jnp.arange(t, dtype=jnp.float32)
    f32 = jnp.float32
    for l in range(DEPTH):
        mod = jax.nn.silu(c) @ ada_w[l] + ada_b[l]
        shift_a, scale_a, gate_a, shift_m, scale_m, gate_m = jnp.split(mod, N_MOD, axis=-1)
        h = modulate(rmsnorm(x, norm_mix_w[l]), shift_a, scale_a)
        proj = (h @ w_in[l]).astype(f32)
        mixed = token_mix(proj, positions, conv_w[l].astype(f32), a_log[l].astype(f32),
                          dt_bias[l].astype(f32), ret_norm_w[l].astype(f32),
                          gdn_norm_w[l].astype(f32)).astype(x.dtype)
        x = x + gate_a[:, None, :] * (mixed @ w_out[l])
        h = modulate(rmsnorm(x, norm_mlp_w[l]), shift_m, scale_m)
        x = x + gate_m[:, None, :] * (jnp.square(jax.nn.relu(h @ w_ff1[l])) @ w_ff2[l])
    return rmsnorm(x, norm_final_w)


_drawn_inputs = setup_inputs


def setup_inputs(seed=0):
    import zlib

    import numpy as np

    out = dict(_drawn_inputs(seed))
    spreads = {}
    factors = {'norm_mix_w': 8.0,
     'a_log': 2.884,
     'ret_norm_w': 28.47,
     'gdn_norm_w': 27.304,
     'norm_mlp_w': 21.592,
     'norm_final_w': 7.884}
    for name, (base, spread) in spreads.items():
        noise = np.random.default_rng([zlib.crc32(name.encode()), seed]).standard_normal(out[name].shape)
        drawn = base * np.exp(spread * noise) if base else spread * noise
        out[name] = __import__('jax').numpy.asarray(drawn.astype(out[name].dtype))
    for name, factor in factors.items():
        out[name] = (out[name] * factor).astype(out[name].dtype)
    return out
```

```python
from contextlib import ExitStack

import numpy as np

import concourse.bass as bass
from concourse import mybir

ACT = mybir.ActivationFunctionType
ALU = mybir.AluOpType
AX = mybir.AxisListType
F32 = mybir.dt.float32
F32R = mybir.dt.float32r

P = 128
D = 1024
SEQ = 2048
NT = 512
NB = SEQ // NT
KT = D // P
HEADS = 4
SUB = NT // P
CHUNK = 64
FF = 4 * D
EPS = 1e-6
DK = 128
TAPS = 4
HIST = TAPS - 1
UNIT = 8
GK, GQ, GV, RK, RQ, RV, RG, GZ = range(UNIT)
FFG = 4
NG = FF // P // FFG
TILES_PER_BLOCK = HEADS * UNIT + KT + NG * 2 * FFG
NRAW = 2
HALVES = 4
LEVELS = 7
PAR_MASK = 32
PAR = PAR_MASK + P
(C_RETW, C_GDNW, C_QDEC, C_KDEC, C_SDEC) = range(12, 17)

SEMAPHORES = """
const_in lmask_in cs_in par_in mod_par_in host_consts
raw0 raw1 w_hi w_lo w_used
ada0 ada1 ada2 ada3 silu_c ada_sums mod_cols mod_ready
sq_ready sq_added colsum_ready ms_ready rstd_ready diag_ready row_ready row_kept xn_ready
hf_ready h_hi h_lo
wg_split gate_out gate_steps gate_exp
proj_evac out_evac ff1_relu ff1_evac hid_hi hid_lo ff2_evac
unit_start conv_steps tanh_k tanh_q tanh_v tanh_rg tanh_gz y_k y_q y_v y_rg y_gz
swap_k swap_q rot_cos_k rot_sin_k rot_cos_q rot_sin_q rot_k rot_q
gstrict d_out gc_out d_exp gc_exp d_mask beta_d
rt_out kdec_r v_r s_out s_masked r_upd r_cross r_state
gt_out sqk_ready sqq_ready ss_steps nk_ready k_nat kt_out kt_ready v_nat
kk_out attn_ready lt_ready lvl_mask u_first t_first_out t_ready x_out x_ready y_out t_next u_next
negc_ready gfac gvar rvar sr_kept silu_v mod_steps gates_done kd_ready ks_out r_ready tr_out vnew_ready upd_out g_state o2_out
ro_steps rsq rpow ro_t go_steps gsq gpow go_t
mix_r mix_g state_kept
o_ready o_dma0 o_dma1 o_dma2 o_dma3 x1_in
""".split()


def build(nc, xT, w_all, w_gate, ada_w, c_col, ada_b, norms, par, masks, cos, sin, gate_par, out):
    ctx = ExitStack()
    with ctx:
        def sb(name, shape, dt=F32):
            return ctx.enter_context(nc.sbuf_tensor(name, shape, dt))

        S = {n: ctx.enter_context(nc.semaphore(n)) for n in SEMAPHORES}

        hT = sb("hT", [P, 2, KT, NT], F32R)
        mT = sb("mT", [P, 2, KT, NT], F32R)
        w2 = sb("w2", [P, 2, HALVES, 4 * P], F32R)
        raw = sb("raw", [P, NRAW, KT * P])
        x1 = sb("x1", [P, KT, NT])
        hidden_ctx = nc.sbuf_tensor("hid", [P, 2, 2, FFG, NT], F32R)
        hid = hidden_ctx.__enter__()
        hidden_ctx.__exit__(None, None, None)
        mixing = sb("mixing", [P, 16, NT])
        (yk, yq, yv, sqk, sqq, knat, kT, vnat, gs, Dm, attn, LT,
         th, swp, og, orr) = (mixing[:, i, :] for i in range(16))
        T, U, X, Lm, bD = yk, yv, sqk, sqq, gs
        pg = sb("pg", [P, 3, HIST + NT])
        pr = sb("pr", [P, 5, NT])
        gts = sb("gts", [P, 2, NT])
        rot = sb("rot", [P, 2, NT])
        rs = sb("rs", [P, 3, NT])
        io = sb("io", [P, 4, NT])
        row1 = sb("row1", [P, NT])
        cs = sb("cs", [P, 2, NT])
        consts = sb("consts", [P, 4, P])
        lmask = sb("lmask", [P, LEVELS, P])
        para = sb("para", [P, HEADS, PAR])
        cur = sb("cur", [P, PAR])
        gb = sb("gb", [P, HEADS, 2 * SUB])
        cgb = sb("cgb", [P, 2 * SUB])
        states = sb("states", [P, 2, HEADS, P])
        Sr = sb("Sr", [P, P])[:, :]
        Sg = sb("Sg", [P, P])[:, :]
        hist = sb("hist", [P, HEADS, 3 * HIST])
        rv_ = sb("rvv", [P, 2, P])
        small = sb("small", [P, 256])
        ab = sb("ab", [P, 48 + 7 * KT + 8 + 48])
        wg = sb("wg", [P, KT, 8])
        wgs = sb("wgs", [P, 2, KT, 8], F32R)

        ident, ones, upper, strict = (consts[:, i, :] for i in range(4))
        mod = ab[:, 0:48]
        A1, B1, GA, A2, B2, GM, WF = (ab[:, 48 + i * KT:48 + (i + 1) * KT] for i in range(7))
        ccol = ab[:, 104:112]
        adab = ab[:, 112:160]
        nrm = small[:, 0:24]
        gpar = small[:, 24:32]
        mhalf = small[:, 240:248]
        ms, rstd = small[:, 36:40], small[:, 40:44]
        negA = small[:, 44:48]
        eg = small[:, 48:60]
        negc = small[:, 60:64]
        ssk, ssq, nk, nq = (small[:, 64 + 4 * i:68 + 4 * i] for i in range(4))
        ss, nkq = small[:, 64:72], small[:, 72:80]
        rme, rva, rrs = (small[:, 80 + 4 * i:84 + 4 * i] for i in range(3))
        gva, grs, gfa, gtm = (small[:, 92 + 4 * i:96 + 4 * i] for i in range(4))
        gx, gu, gz_, gp, gq_ = (small[:, 112 + 16 * i:128 + 16 * i] for i in range(5))
        gbt = small[:, 192:208]
        scol = small[:, 208:216]
        stmp = small[:, 216:224]

        acc = ctx.enter_context(nc.psum_tensor("acc", [P, 2, 512], F32))
        pm = ctx.enter_context(nc.psum_tensor("pm", [P, 6, 512], F32))
        bA, bB, bC, bD_, bE, bF = (pm[:, i, :] for i in range(6))

        block = ctx.enter_context(nc.Block())

        def sub(ap, t):
            return ap[:, t * P:(t + 1) * P]

        def by_sub(ap):
            return ap.rearrange("p (t c) -> p t c", t=SUB)

        def over_tokens(col4):
            return col4.unsqueeze(2).to_broadcast([P, SUB, P])

        def over_subs(m):
            return m.unsqueeze(1).to_broadcast([P, SUB, P])

        sqrow, dg = th, swp
        sqrow_last = mixing[:, 0, :]

        def tile_of(b, phase_tile):
            return UNIT + TILES_PER_BLOCK * b + phase_tile

        def proj_of(b, u):
            return UNIT + HEADS * UNIT * b + UNIT * u

        OUT0 = HEADS * UNIT
        FF0 = OUT0 + KT

        def norm_no(b, which):
            return 1 + 3 * b + which

        OUT0 = HEADS * UNIT
        FF0 = OUT0 + KT
        RAWSEM = (S["raw0"], S["raw1"])
        ADASEM = (S["ada0"], S["ada1"], S["ada2"], S["ada3"])
        ada_at = [k % 4 for k in range(KT)] + [k % 3 for k in range(2 * KT)]
        ada_turn = [ada_at[:k].count(ada_at[k]) for k in range(3 * KT)]
        OSEM = (S["o_dma0"], S["o_dma1"], S["o_dma2"], S["o_dma3"])
        GSTEPS = 19
        ff_pairs = NG // 2 - 1

        def quarter_of(b, t):
            return (UNIT + t) // 4 + (TILES_PER_BLOCK // 4) * b

        def ada_slot(k):
            at = 4 * ada_at[k]
            return mixing[:, at:at + 4, :].rearrange("p a n -> p (a n)")

        ada_acc = [x.rearrange("p a n -> p (a n)") for x in (io[:, :, :], x1[:, 0:4, :], x1[:, 4:8, :])]

        @block.sync
        def _(e):
            e.dma_start(ab[:, 104:112], c_col).then_inc(S["mod_par_in"], 16)
            e.dma_start(ab[:, 112:160], ada_b).then_inc(S["mod_par_in"], 16)
            e.dma_start(nrm, norms).then_inc(S["mod_par_in"], 16)
            e.dma_start(gpar, gate_par).then_inc(S["mod_par_in"], 16)
            e.dma_start(consts[:, :, :], masks[:, 0:4, :]).then_inc(S["const_in"], 16)
            e.dma_start(wg[:, :, :], w_gate).then_inc(S["const_in"], 16)
            def load(q, i, index, wait=True):
                if wait:
                    e.wait_ge(S["w_lo"], 8 * q + 2 * (i - NRAW) + 2)
                e.dma_start(raw[:, i % NRAW, :], w_all[index]).then_inc(RAWSEM[i % NRAW], 16)

            for k in range(3 * KT):
                if ada_turn[k]:
                    before = max(j for j in range(k) if ada_at[j] == ada_at[k])
                    e.wait_ge(S["ada_sums"], before + 1)
                e.dma_start(ada_slot(k), ada_w[k // KT, k % KT]).then_inc(ADASEM[ada_at[k]], 16)
                if k == 3:
                    load(0, 0, (HEADS - 1) * UNIT, wait=False)
                    load(0, 1, (HEADS - 1) * UNIT + 1, wait=False)
                    e.dma_start(x1[:, :, :], xT[0]).then_inc(S["x1_in"], 16)
                    e.dma_start(lmask[:, :, :], masks[:, 4:4 + LEVELS, :]).then_inc(S["lmask_in"], 16)
                    e.dma_start(para[:, :, :], par).then_inc(S["par_in"], 16)
                    e.dma_start(cs[:, 0, :], cos[0]).then_inc(S["cs_in"], 16)
                    e.dma_start(cs[:, 1, :], sin[0]).then_inc(S["cs_in"], 16)
                if k in (10, 13, 16, 19):
                    i = 2 + (k - 10) // 3
                    load(i // 4, i % 4, (HEADS - 1) * UNIT + i)

            for i in range(6, UNIT):
                load(i // 4, i % 4, (HEADS - 1) * UNIT + i)
            with e.Fori(0, NB) as b:
                with e.Fori(0, TILES_PER_BLOCK // 4) as q:
                    for i in range(4):
                        load(quarter_of(b, 0) + q, i, q * 4 + i)
            for i in range(2):
                load(quarter_of(NB, 0), i, i)

        @block.tensor
        def _(e):
            def step(q, i, half, k, x, bank, first, last):
                local = 2 * i + half
                if k == 0:
                    e.wait_ge(S["w_lo"], 8 * q + local + 1)
                slot = local % HALVES
                whi = w2[:, 0, slot, k * P:(k + 1) * P]
                wlo = w2[:, 1, slot, k * P:(k + 1) * P]
                e.matmul(bank, whi, x[:, 0, :], start=first, stop=False)
                e.matmul(bank, whi, x[:, 1, :], start=False, stop=False)
                m = e.matmul(bank, wlo, x[:, 0, :], start=False, stop=last)
                return m.then_inc(S["w_used"], 1) if k == 3 else m

            def stats(n, sqrow=sqrow):
                e.wait_ge(S["sq_added"], (KT - 1) * (n + 1))
                for t in range(SUB):
                    m = e.matmul(bB[:, 2 * t:2 * t + 2], sub(sqrow, t), ones[:, 0:2], start=True, stop=True)
                m.then_inc(S["colsum_ready"], 1)
                e.wait_ge(S["diag_ready"], n + 1)
                e.matmul(bA, ones, dg, start=True, stop=True).then_inc(S["row_ready"], 1)

            def gate_columns(m, hn):
                e.wait_ge(S["h_lo"], KT * (hn + 1))
                for t in range(SUB):
                    o = bB[:, 32 + 8 * t:40 + 8 * t]
                    for k in range(KT):
                        hi, lo = hT[:, 0, k, t * P:(t + 1) * P], hT[:, 1, k, t * P:(t + 1) * P]
                        e.matmul(o, hi, wgs[:, 0, k, :], start=k == 0, stop=False)
                        e.matmul(o, hi, wgs[:, 1, k, :], start=False, stop=False)
                        mm = e.matmul(o, lo, wgs[:, 0, k, :], start=False, stop=k == KT - 1)
                mm.then_inc(S["gate_out"], 1)

            def four(bank, lhs, rhs):
                for t in range(SUB):
                    m = e.matmul(sub(bank, t), sub(lhs, t), sub(rhs, t), start=True, stop=True)
                return m

            def turn(bank, x):
                for t in range(SUB):
                    m = e.transpose(sub(bank, t), sub(x, t), ident)
                return m

            def unit(b, u, n, q, pt, new_h=False):
                e.wait_ge(S["proj_evac"], pt)
                e.wait_ge(S["ff2_evac"], 2 * NG * FFG * b)
                for s in range(UNIT * KT):
                    i, k = s // KT, s % KT
                    if k == 0 and i >= 2:
                        e.wait_ge(S["proj_evac"], pt + i - 1)
                    if new_h and i == 0:
                        e.wait_ge(S["h_lo"], KT * (1 + 2 * b) + k + 1)
                    step(q + i // 4, i % 4, k // 4, k % 4, hT[:, :, k, :], acc[:, i % 2, :],
                             k == 0, k == KT - 1)
                    if s == 3:
                        e.wait_ge(S["gstrict"], n + 1)
                        for t in range(SUB):
                            m = e.matmul(sub(bA, t), sub(gs, t), upper, start=True, stop=True)
                        m.then_inc(S["d_out"], 1)
                        for j, w in enumerate((upper, strict, ones)):
                            m = e.matmul(bB[:, 4 * j:4 * j + 4], w, cgb[:, 0:SUB], start=True, stop=True)
                        m.then_inc(S["gc_out"], 1)
                    if s == 8:
                        e.wait_ge(S["rot_k"], n + 1)
                        e.wait_ge(S["mix_r"], 3 * n)
                        turn(bC, rot[:, 0, :])
                        turn(bD_, pr[:, RV - RK, :]).then_inc(S["rt_out"], 1)
                    if s == 11:
                        e.wait_ge(S["y_k"], n + 1)
                        e.wait_ge(S["y_q"], n + 1)
                        e.wait_ge(S["y_v"], n + 1)
                        e.wait_ge(S["gc_exp"], n + 1)
                        e.wait_ge(S["mix_g"], 3 * n)
                        turn(bE, yk)
                        turn(bF, yq)
                        turn(bB, yv).then_inc(S["gt_out"], 1)
                    if s == 13:
                        e.wait_ge(S["rot_q"], n + 1)
                        e.wait_ge(S["d_exp"], n + 1)
                        four(bA, rot[:, 0, :], rot[:, 1, :]).then_inc(S["s_out"], 1)
                    if s == 15:
                        e.wait_ge(S["k_nat"], n + 1)
                        turn(bE, knat).then_inc(S["kt_out"], 1)
                    if s == 16:
                        e.wait_ge(S["kdec_r"], n + 1)
                        e.wait_ge(S["v_r"], n + 1)
                        e.wait_ge(S["s_masked"], n + 1)
                        four(bA, rs[:, 0, :], rs[:, 1, :])
                        four(bD_, rs[:, 2, :], rs[:, 1, :]).then_inc(S["r_upd"], 1)
                    if s in (16, 19, 23, 27):
                        t = (16, 19, 23, 27).index(s)
                        if t:
                            e.wait_ge(S["r_state"], 3 * n + t)
                        e.matmul(sub(bC, t), sub(rot[:, 1, :], t), Sr, start=True, stop=True).then_inc(S["r_cross"], 1)
                    if s == 17:
                        e.wait_ge(S["kt_ready"], n + 1)
                        e.wait_ge(S["v_nat"], n + 1)
                        e.wait_ge(S["sqq_ready"], n + 1)
                        four(bB, kT, kT)
                        four(bF, kT, yq).then_inc(S["kk_out"], 1)
                    if s == 20:
                        e.wait_ge(S["u_first"], n + 1)
                        turn(bE, U).then_inc(S["t_first_out"], 1)
                    if 22 <= s <= 42 and s % 4 == 2:
                        l = (s - 22) // 4 + 1
                        e.wait_ge(S["lvl_mask"], LEVELS * n + l + 1)
                        if l == 1:
                            e.wait_ge(S["t_ready"], n + 1)
                        else:
                            e.wait_ge(S["t_next"], (LEVELS - 2) * n + l - 1)
                        four(bE, Lm, T).then_inc(S["x_out"], 1)
                    if 24 <= s <= 44 and s % 4 == 0:
                        l = (s - 24) // 4 + 1
                        e.wait_ge(S["x_ready"], (LEVELS - 1) * n + l)
                        if l > 1:
                            e.wait_ge(S["u_next"], (LEVELS - 1) * n + l - 1)
                        else:
                            e.wait_ge(S["attn_ready"], n + 1)
                            e.wait_ge(S["lt_ready"], n + 1)
                        m = four(bF, X, U)
                        if l < LEVELS - 1:
                            m = four(bB, U, X)
                        m.then_inc(S["y_out"], 1)
                    if s == 35:
                        e.wait_ge(S["ro_steps"], 6 * n + 6)
                        turn(bC, orr).then_inc(S["ro_t"], 1)
                    if s in range(46, 62, 4):
                        t = (s - 46) // 4
                        if t == 0:
                            e.wait_ge(S["u_next"], (LEVELS - 1) * (n + 1))
                        else:
                            e.wait_ge(S["g_state"], SUB * n + t)
                        e.matmul(sub(bB, t), sub(kT, t), Sg, start=True, stop=True).then_inc(S["ks_out"], 1)
                        e.matmul(sub(bF, t), sub(yq, t), Sg, start=True, stop=True)
                    if s in range(47, 63, 4):
                        t = (s - 47) // 4
                        e.wait_ge(S["r_ready"], SUB * n + t + 1)
                        e.matmul(sub(bE, t), sub(U, t), rv_[:, 0, :], start=True, stop=True).then_inc(S["tr_out"], 1)
                    if s in range(49, 65, 4):
                        t = (s - 49) // 4
                        e.wait_ge(S["vnew_ready"], SUB * n + t + 1)
                        if t == 0:
                            e.wait_ge(S["kd_ready"], n + 1)
                            e.wait_ge(S["ro_steps"], 6 * n + 6)
                        e.matmul(sub(bD_, t), sub(knat, t), rv_[:, 1, :], start=True, stop=True).then_inc(S["upd_out"], 1)
                        e.matmul(sub(bA, t), sub(attn, t), rv_[:, 1, :], start=True, stop=True).then_inc(S["o2_out"], 1)
                if new_h:
                    e.wait_ge(S["r_ready"], SUB * (n + 1))
                    gate_columns(b + 1, 1 + 2 * b)
                e.wait_ge(S["go_steps"], 6 * n + 6)
                turn(bE, og).then_inc(S["go_t"], 1)

            e.wait_ge(S["const_in"], 32)
            def mod_columns(g, bank):
                e.wait_ge(S["ada_sums"], KT * (g + 1))
                for j in range(16):
                    m = e.matmul(bank[:, 2 * (16 * g + j):2 * (16 * g + j) + 2], ada_acc[g][:, j * P:(j + 1) * P],
                                 ones[:, 0:2], start=True, stop=True)
                m.then_inc(S["mod_cols"], 1)

            mod_columns(0, bC)
            stats(0)
            e.wait_ge(S["wg_split"], 2)
            gate_columns(0, 0)
            for s in range(UNIT * KT):
                i, k = s // KT, s % KT
                if k == 0 and i >= 2:
                    e.wait_ge(S["proj_evac"], i - 1)
                step(i // 4, i % 4, k // 4, k % 4, hT[:, :, k, :], acc[:, i % 2, :], k == 0, k == KT - 1)
            mod_columns(1, bC)
            mod_columns(2, bC)
            e.wait_ge(S["mod_ready"], 2)
            e.wait_ge(S["par_in"], 16)
            e.wait_ge(S["const_in"], 32)
            e.wait_ge(S["lmask_in"], 16)

            with e.Fori(0, NB) as b:
                with e.Fori(0, HEADS - 2) as u:
                    unit(b, u, b * HEADS + u, quarter_of(b, 0) + u * (UNIT // 4), proj_of(b, u))
                e.wait_ge(S["mix_g"], 3 * (HEADS * b + HEADS - 2))
                stats(norm_no(b, 0))
                e.wait_ge(S["row_kept"], b + 1)
                unit(b, HEADS - 2, b * HEADS + HEADS - 2, quarter_of(b, (HEADS - 2) * UNIT), proj_of(b, HEADS - 2))
                unit(b, HEADS - 1, b * HEADS + HEADS - 1, quarter_of(b, (HEADS - 1) * UNIT), proj_of(b, HEADS - 1),
                     new_h=True)

                e.wait_ge(S["mix_r"], 3 * HEADS * (b + 1))
                e.wait_ge(S["mix_g"], 3 * HEADS * (b + 1))
                e.wait_ge(S["proj_evac"], proj_of(b, HEADS))
                for j in range(KT):
                    if j >= 2:
                        e.wait_ge(S["out_evac"], KT * b + j - 1)
                    for k in range(KT):
                        step(quarter_of(b, OUT0) + j // 4, j % 4, k // 4, k % 4, mT[:, :, k, :],
                                 acc[:, j % 2, :], k == 0, k == KT - 1)
                e.wait_ge(S["gates_done"], b + 2)
                stats(norm_no(b, 1))

                def ff1(q, g, par, after):
                    for i in range(FFG):
                        if i >= 2 or after == "ff1":
                            e.wait_ge(S["ff1_evac"], NG * FFG * b + FFG * g + i - 1)
                        elif after == "ff2":
                            e.wait_ge(S["ff2_evac"], 2 * NG * FFG * b + 2 * FFG * (g - 1) - 1 + i)
                        else:
                            e.wait_ge(S["out_evac"], KT * (b + 1))
                        for k in range(KT):
                            if after == "out" and i == 0:
                                e.wait_ge(S["h_lo"], KT * (2 + 2 * b) + k + 1)
                            step(q, i, k // 4, k % 4, mT[:, :, k, :], acc[:, i % 2, :], k == 0, k == KT - 1)

                def ff2(q, g, par, after):
                    e.wait_ge(S["hid_lo"], NG * FFG * b + FFG * (g + 1))
                    for o in range(2 * FFG):
                        if o >= 2 or after == "ff2":
                            e.wait_ge(S["ff2_evac"], 2 * NG * FFG * b + 2 * FFG * g + o - 1)
                        else:
                            e.wait_ge(S["ff1_evac"], NG * FFG * b + FFG * (g + 2) - 1 + o)
                        for k in range(FFG):
                            step(q, o // 2, o % 2, k, hid[:, par, :, k, :], acc[:, o % 2, :], k == 0, k == FFG - 1)

                ffq = quarter_of(b, FF0)
                ff1(ffq, 0, 0, "out")
                ff1(ffq + 1, 1, 1, "ff1")
                ff2(ffq + 2, 0, 0, "ff1")
                with e.Fori(0, ff_pairs) as r:
                    ff1(ffq + 3 + 4 * r, 2 * r + 2, 0, "ff2")
                    ff2(ffq + 4 + 4 * r, 2 * r + 1, 1, "ff1")
                    ff1(ffq + 5 + 4 * r, 2 * r + 3, 1, "ff2")
                    ff2(ffq + 6 + 4 * r, 2 * r + 2, 0, "ff1")
                ff2(ffq + 2 * NG - 1, NG - 1, 1, "ff2")
                stats(norm_no(b, 2), sqrow_last)

        @block.scalar
        def _(e):
            def hi(q, local):
                tile = local // 2
                e.wait_ge(RAWSEM[tile % NRAW], 16 * (2 * q + tile // NRAW + 1))
                if not isinstance(q, int) or 8 * q + local >= HALVES:
                    e.wait_ge(S["w_used"], 8 * q + local - HALVES + 1)
                e.activation(w2[:, 0, local % HALVES, :], raw[:, tile % NRAW, local % 2 * NT:(local % 2 + 1) * NT],
                             ACT.Copy).then_inc(S["w_hi"], 1)

            def io_written(b):
                for q in OSEM:
                    e.wait_ge(q, 32 * b)

            def square(n, j, sqrow=sqrow):
                if j >= 3:
                    e.wait_ge(S["sq_added"], (KT - 1) * n + j - 2)
                dst = sqrow if j == 0 else io[:, j % 2, :]
                e.activation(dst, x1[:, j, :], ACT.Square).then_inc(S["sq_ready"], 1)

            def modulated(hn, dst, A, B, used, count):
                e.wait_ge(used, count)
                for j in range(KT):
                    e.wait_ge(S["xn_ready"], KT * hn + j + 1)
                    if j >= 2:
                        e.wait_ge(S["h_lo"], KT * hn + j - 1)
                    e.activation(io[:, 2 + j % 2, :], io[:, j % 2, :], ACT.Identity, scale=A[:, j:j + 1],
                                 bias=B[:, j:j + 1]).then_inc(S["hf_ready"], 1)
                    e.wait_ge(S["hf_ready"], KT * hn + j + 1)
                    e.activation(dst[:, 0, j, :], io[:, 2 + j % 2, :], ACT.Copy).then_inc(S["h_hi"], 1)

            def gate_exps(m):
                e.wait_ge(S["gate_steps"], GSTEPS * m + 3)
                e.activation(gu, gu, ACT.Exp, scale=-1.0).then_inc(S["gate_exp"], 1)
                e.activation(gbt, gbt, ACT.Exp, scale=-1.0).then_inc(S["gate_exp"], 1)

            def evac(n, q, i):
                e.wait_ge(S["w_used"], 8 * q + 2 * i + 2)
                if n is not None:
                    if i < 3:
                        e.wait_ge(S["conv_steps"], 12 * n + 4 * (i + 1))
                    elif i == RK or i == RQ:
                        e.wait_ge(S["rot_cos_k"] if i == RK else S["rot_cos_q"], n + 1)
                        e.wait_ge(S["swap_k"] if i == RK else S["swap_q"], 2 * n + 2)
                    elif i == RV:
                        e.wait_ge(S["rt_out"], n + 1)
                    else:
                        e.wait_ge(S["y_rg"] if i == RG else S["y_gz"], n + 1)
                dst = pg[:, i, HIST:HIST + NT] if i < 3 else pr[:, i - 3, :]
                e.activation(dst, acc[:, i % 2, :], ACT.Copy).then_inc(S["proj_evac"], 1)

            def unit(b, n, q, pt, rows=0):
                e.wait_ge(S["w_used"], 8 * quarter_of(b, 0))
                for s in range(UNIT * KT):
                    if s % 4 == 0:
                        hi(q, s // 4 + 3)
                    if s % 8 == 0 and s:
                        evac(n, q, s // 8 - 1)
                    if s == 1:
                        e.wait_ge(S["proj_evac"], pt)
                        e.wait_ge(S["ro_steps"], 6 * n)
                        if rows:
                            e.wait_ge(S["row_kept"], b + 1)
                        e.activation(swp[0:64, :], pr[64:128, 0, :], ACT.Copy).then_inc(S["swap_k"], 1)
                        e.activation(swp[64:128, :], pr[0:64, 0, :], ACT.Copy).then_inc(S["swap_k"], 1)
                    if s == 2:
                        e.wait_ge(S["conv_steps"], 12 * n + 4)
                        e.activation(th, yk, ACT.Tanh, scale=0.5).then_inc(S["tanh_k"], 1)
                    if s == 4:
                        e.wait_ge(S["d_out"], n + 1)
                        e.activation(Dm, bA, ACT.Exp).then_inc(S["d_exp"], 1)
                        e.wait_ge(S["gc_out"], n + 1)
                        e.activation(eg, bB[:, 0:12], ACT.Exp).then_inc(S["gc_exp"], 1)
                    if s == 5:
                        e.wait_ge(S["rot_k"], n + 1)
                        e.activation(swp[0:64, :], pr[64:128, 1, :], ACT.Copy).then_inc(S["swap_q"], 1)
                        e.activation(swp[64:128, :], pr[0:64, 1, :], ACT.Copy).then_inc(S["swap_q"], 1)
                    if s == 6:
                        e.wait_ge(S["conv_steps"], 12 * n + 8)
                        e.activation(og, yq, ACT.Tanh, scale=0.5).then_inc(S["tanh_q"], 1)
                    if s == 7:
                        e.wait_ge(S["conv_steps"], 12 * n + 12)
                        e.activation(orr, yv, ACT.Tanh, scale=0.5).then_inc(S["tanh_v"], 1)
                    if s == 9:
                        e.wait_ge(S["rt_out"], n + 1)
                        e.activation(rs[:, 0, :], bC, ACT.Copy, scale=cur[:, C_KDEC:C_KDEC + 1]).then_inc(S["kdec_r"], 1)
                        e.activation(rs[:, 1, :], bD_, ACT.Copy).then_inc(S["v_r"], 1)
                    if s == 12:
                        e.wait_ge(S["gt_out"], n + 1)
                        e.activation(sqk, bE, ACT.Square).then_inc(S["sqk_ready"], 1)
                        e.activation(sqq, bF, ACT.Square).then_inc(S["sqq_ready"], 1)
                        e.activation(vnat, bB, ACT.Copy, scale=0.5).then_inc(S["v_nat"], 1)
                    if s == 14:
                        e.activation(gts[:, 0, :], pr[:, RG - RK, :], ACT.Tanh, scale=0.5).then_inc(S["tanh_rg"], 1)
                        e.activation(gts[:, 1, :], pr[:, GZ - RK, :], ACT.Tanh, scale=0.5).then_inc(S["tanh_gz"], 1)
                    if s == 15:
                        e.wait_ge(S["kt_out"], n + 1)
                        e.activation(kT, bE, ACT.Copy).then_inc(S["kt_ready"], 1)
                    if s == 20:
                        e.wait_ge(S["t_first_out"], n + 1)
                        e.activation(T, bE, ACT.Copy).then_inc(S["t_ready"], 1)
                    if 22 <= s <= 42 and s % 4 == 2:
                        l = (s - 22) // 4 + 1
                        e.wait_ge(S["x_out"], (LEVELS - 1) * n + l)
                        if l > 1:
                            e.wait_ge(S["y_out"], (LEVELS - 1) * n + l - 1)
                        e.activation(X, bE, ACT.Copy).then_inc(S["x_ready"], 1)
                    if s == 31:
                        e.wait_ge(S["ro_steps"], 6 * n + 4)
                        e.activation(th, orr, ACT.Square).then_inc(S["rsq"], 1)
                    if s in range(47, 63, 4):
                        t = (s - 47) // 4
                        e.wait_ge(S["tr_out"], SUB * n + t + 1)
                        if t:
                            e.wait_ge(S["o2_out"], SUB * n + t)
                        e.activation(rv_[:, 1, :], sub(bE, t), ACT.Copy,
                                     scale=cgb[:, SUB + t:SUB + t + 1]).then_inc(S["vnew_ready"], 1)
                evac(n, q, UNIT - 1)
                e.wait_ge(S["go_steps"], 6 * n + 2)
                e.activation(sqk, og, ACT.Square).then_inc(S["gsq"], 1)

            e.wait_ge(S["mod_par_in"], 64)
            e.activation(scol, ccol, ACT.Exp, scale=-1.0).then_inc(S["silu_c"], 1)
            e.activation(negA, gpar[:, 0:4], ACT.Exp).then_inc(S["silu_c"], 1)
            e.wait_ge(S["const_in"], 32)
            e.activation(wgs[:, 0, :, :], wg[:, :, :], ACT.Copy).then_inc(S["wg_split"], 1)
            for h in range(3):
                hi(0, h)
            e.wait_ge(S["x1_in"], 16)
            e.wait_ge(S["mod_cols"], 1)
            for j in range(KT):
                square(0, j)
            modulated(0, hT, A1, B1, S["mod_ready"], 1)
            for i in range(UNIT):
                hi(0, 2 * i + 3)
                hi(0, 2 * i + 4)
                evac(None, 0, i)
                if i == 0:
                    gate_exps(0)

            with e.Fori(0, NB) as b:
                e.wait_ge(S["o_ready"], KT * b)
                e.wait_ge(S["mod_cols"], 3)
                e.dma_start(x1[:, :, :], xT[(b + 1) % NB]).then_inc(S["x1_in"], 16)
                with e.Fori(0, HEADS - 2) as u:
                    unit(b, b * HEADS + u, quarter_of(b, 0) + u * (UNIT // 4), proj_of(b, u))
                e.wait_ge(S["x1_in"], 32 + 32 * b)
                io_written(b)
                for j in range(KT):
                    square(norm_no(b, 0), j)
                unit(b, b * HEADS + HEADS - 2, quarter_of(b, (HEADS - 2) * UNIT), proj_of(b, HEADS - 2), rows=1)
                modulated(1 + 2 * b, hT, A1, B1, S["w_used"], 8 * quarter_of(b, (HEADS - 1) * UNIT))
                e.wait_ge(S["xn_ready"], KT * (2 + 2 * b))
                e.dma_start(x1[:, :, :], xT[b]).then_inc(S["x1_in"], 16)
                unit(b, b * HEADS + HEADS - 1, quarter_of(b, (HEADS - 1) * UNIT), proj_of(b, HEADS - 1))
                gate_exps(b + 1)
                e.wait_ge(S["rot_q"], HEADS * (b + 1))
                e.dma_start(cs[:, 0, :], cos[(b + 1) % NB]).then_inc(S["cs_in"], 16)
                e.dma_start(cs[:, 1, :], sin[(b + 1) % NB]).then_inc(S["cs_in"], 16)
                for j in range(KT):
                    hi(quarter_of(b, OUT0), 2 * j + 3)
                    if j:
                        e.wait_ge(S["out_evac"], KT * b + j)
                        square(norm_no(b, 1), j - 1)
                    hi(quarter_of(b, OUT0), 2 * j + 4)
                e.wait_ge(S["out_evac"], KT * (b + 1))
                square(norm_no(b, 1), KT - 1)
                modulated(2 + 2 * b, mT, A2, B2, S["w_used"], 8 * quarter_of(b, FF0))

                def ff1(q, g, par):
                    for i in range(FFG):
                        f = NG * FFG * b + FFG * g + i
                        hi(q, 2 * i + 3)
                        hi(q, 2 * i + 4)
                        e.wait_ge(S["w_used"], 8 * q + 2 * i + 2)
                        if i >= 2:
                            e.wait_ge(S["ff1_evac"], f - 1)
                        e.activation(io[:, i % 2, :], acc[:, i % 2, :], ACT.Relu).then_inc(S["ff1_relu"], 1)
                        if i == 0:
                            e.wait_ge(S["w_used"], 8 * q)
                        e.wait_ge(S["ff1_evac"], f + 1)
                        e.activation(hid[:, par, 0, i, :], io[:, 2 + i % 2, :], ACT.Copy).then_inc(S["hid_hi"], 1)

                def ff2(q):
                    for i in range(FFG):
                        hi(q, 2 * i + 3)
                        hi(q, 2 * i + 4)

                ffq = quarter_of(b, FF0)
                ff1(ffq, 0, 0)
                ff1(ffq + 1, 1, 1)
                ff2(ffq + 2)
                with e.Fori(0, ff_pairs) as r:
                    ff1(ffq + 3 + 4 * r, 2 * r + 2, 0)
                    ff2(ffq + 4 + 4 * r)
                    ff1(ffq + 5 + 4 * r, 2 * r + 3, 1)
                    ff2(ffq + 6 + 4 * r)
                for o in range(KT):
                    hi(ffq + 2 * NG - 1, o + 3)
                    if o:
                        e.wait_ge(S["ff2_evac"], 2 * NG * FFG * (b + 1) - KT + o)
                        square(norm_no(b, 2), o - 1, sqrow_last)
                e.wait_ge(S["ff2_evac"], 2 * NG * FFG * (b + 1))
                square(norm_no(b, 2), KT - 1, sqrow_last)
                for j in range(KT):
                    e.wait_ge(S["o_ready"], KT * b + j + 1)
                    e.dma_start(out[b, :, j, :], io[:, j % 4, :]).then_inc(OSEM[j % 4], 16)
            for q in OSEM:
                e.wait_ge(q, 32 * NB)

        @block.vector
        def _(e):
            one = 1.0

            def row_of(n):
                e.wait_ge(S["colsum_ready"], n + 1)
                e.tensor_scalar(ms, bB[:, 0:2 * SUB:2], 1.0 / D, EPS, ALU.mult, ALU.add).then_inc(S["ms_ready"], 1)
                e.wait_ge(S["rstd_ready"], n + 1)
                e.tensor_tensor(by_sub(dg), over_subs(ident), over_tokens(rstd), ALU.mult).then_inc(S["diag_ready"], 1)
                e.wait_ge(S["row_ready"], n + 1)

            def add_square(n, j, sqrow=sqrow):
                e.wait_ge(S["sq_ready"], KT * n + j + 1)
                if j > 1:
                    e.wait_ge(S["sq_added"], (KT - 1) * n + j - 1)
                e.tensor_tensor(sqrow, sqrow, io[:, j % 2, :], ALU.add).then_inc(S["sq_added"], 1)

            def normed(n, hn, row):
                e.wait_ge(S["sq_added"], (KT - 1) * (n + 1))
                for j in range(KT):
                    if j >= 2:
                        e.wait_ge(S["hf_ready"], KT * hn + j - 1)
                    e.tensor_tensor(io[:, j % 2, :], x1[:, j, :], row, ALU.mult).then_inc(S["xn_ready"], 1)

            def gates(m):
                done = [0]

                def go(ins):
                    ins.then_inc(S["gate_steps"], 1)
                    done[0] += 1

                def after(k=None):
                    e.wait_ge(S["gate_steps"], GSTEPS * m + (done[0] if k is None else k))

                def ht(x16):
                    return x16.rearrange("p (h t) -> p h t", t=SUB)

                raw8 = bB[:, 32:64].rearrange("p (t c) -> p c t", c=8)
                e.wait_ge(S["gate_out"], m + 1)
                go(e.tensor_tensor(ht(gx), raw8[:, 0:4, :], gpar[:, 4:8].unsqueeze(2).to_broadcast([P, 4, SUB]), ALU.add))
                go(e.tensor_copy(ht(gbt), raw8[:, 4:8, :]))
                after(1)
                go(e.scalar_tensor_tensor(out=gu, in0=gx, scalar=-1.0, in1=gx, op0=ALU.mult, op1=ALU.max))
                e.wait_ge(S["gate_exp"], 2 * m + 2)
                go(e.tensor_scalar(gbt, gbt, one, None, ALU.add))
                after()
                go(e.reciprocal(gb[:, :, SUB:2 * SUB], ht(gbt)))
                go(e.tensor_scalar(gz_, gu, 2.0, None, ALU.add))
                after()
                go(e.reciprocal(gz_, gz_))
                after()
                go(e.tensor_tensor(gz_, gz_, gu, ALU.mult))
                after()
                go(e.tensor_tensor(gp, gz_, gz_, ALU.mult))
                after()
                go(e.tensor_scalar(gq_, gp, 1.0 / 15, None, ALU.mult))
                for c in (13, 11, 9, 7, 5, 3):
                    after()
                    go(e.scalar_tensor_tensor(out=gq_, in0=gq_, scalar=1.0 / c, in1=gp, op0=ALU.add, op1=ALU.mult))
                after()
                go(e.scalar_tensor_tensor(out=gq_, in0=gq_, scalar=one, in1=gz_, op0=ALU.add, op1=ALU.mult))
                after()
                go(e.tensor_scalar(gq_, gq_, 2.0, None, ALU.mult))
                after()
                go(e.scalar_tensor_tensor(out=gq_, in0=gx, scalar=0.0, in1=gq_, op0=ALU.max, op1=ALU.add))
                assert done[0] == GSTEPS
                after()
                e.tensor_tensor(gb[:, :, 0:SUB], ht(gq_), negA.unsqueeze(2).to_broadcast([P, 4, SUB]),
                                ALU.mult).then_inc(S["gates_done"], 1)

            def unit_start(b, u, n):
                e.wait_ge(S["gates_done"], b + 1)
                e.wait_ge(S["proj_evac"], proj_of(b, u))
                e.wait_ge(S["state_kept"], 2 * n)
                e.wait_ge(S["mix_g"], 3 * n)
                e.tensor_scalar(cur[:, :], para[:, u, :], one, None, ALU.mult).then_inc(S["unit_start"], 1)
                e.tensor_scalar(cgb[:, :], gb[:, u, :], one, None, ALU.mult).then_inc(S["unit_start"], 1)
                e.tensor_scalar(Sr[:, :], states[:, 0, u, :], one, None, ALU.mult).then_inc(S["unit_start"], 1)
                e.tensor_scalar(Sg[:, :], states[:, 1, u, :], one, None, ALU.mult).then_inc(S["unit_start"], 1)
                h3 = hist[:, u, :].rearrange("p (a c) -> p a c", a=3)
                e.tensor_scalar(pg[:, :, 0:HIST], h3, one, None, ALU.mult).then_inc(S["unit_start"], 1)
                e.wait_ge(S["unit_start"], 6 * n + 5)
                e.tensor_scalar(h3, pg[:, :, NT:NT + HIST], one, None, ALU.mult).then_inc(S["unit_start"], 1)
                e.wait_ge(S["unit_start"], 6 * n + 6)

            def conv(n, i, y):
                e.tensor_scalar(y, pg[:, i, 0:NT], cur[:, 4 * i:4 * i + 1], None, ALU.mult).then_inc(S["conv_steps"], 1)
                for j in range(1, TAPS):
                    e.wait_ge(S["conv_steps"], 12 * n + 4 * i + j)
                    e.scalar_tensor_tensor(out=y, in0=pg[:, i, j:j + NT], scalar=cur[:, 4 * i + j:4 * i + j + 1],
                                           in1=y, op0=ALU.mult, op1=ALU.add).then_inc(S["conv_steps"], 1)

            def twice_silu(tanh, n, y, t, x, done):
                e.wait_ge(tanh, n + 1)
                e.scalar_tensor_tensor(out=y, in0=t, scalar=one, in1=x, op0=ALU.add, op1=ALU.mult).then_inc(done, 1)

            def rotate(n, i, swap, sin_, cos_, done):
                e.wait_ge(swap, 2 * n + 2)
                e.tensor_tensor(swp, swp, cs[:, 1, :], ALU.mult).then_inc(sin_, 1)
                e.wait_ge(sin_, n + 1)
                e.wait_ge(cos_, n + 1)
                e.tensor_tensor(rot[:, i, :], rot[:, i, :], swp, ALU.add).then_inc(done, 1)

            def mixed(n, sem, bank, w, gate, y, dst):
                e.scalar_tensor_tensor(out=y, in0=bank, scalar=w, in1=gate, op0=ALU.mult, op1=ALU.mult).then_inc(sem, 1)
                e.wait_ge(sem, 3 * n + 1)
                e.tensor_scalar(dst(0), y, one, None, ALU.mult).then_inc(sem, 1)
                e.wait_ge(sem, 3 * n + 2)
                e.tensor_tensor(dst(1), y, dst(0).bitcast(F32), ALU.subtract).then_inc(sem, 1)

            def unit(b, u, n):
                for s in range(UNIT * KT):
                    if s == 0:
                        e.wait_ge(S["cs_in"], 32 + 32 * b)
                        conv(n, GK, yk)
                    if s == 2:
                        twice_silu(S["tanh_k"], n, yk, th, yk, S["y_k"])
                        rotate(n, 0, S["swap_k"], S["rot_sin_k"], S["rot_cos_k"], S["rot_k"])
                        conv(n, GQ, yq)
                        conv(n, GV, yv)
                    if s == 5:
                        e.wait_ge(S["gc_exp"], n + 1)
                        e.tensor_scalar(negc, eg[:, 0:4], -1.0, None, ALU.mult).then_inc(S["negc_ready"], 1)
                    if s == 6:
                        twice_silu(S["tanh_q"], n, yq, og, yq, S["y_q"])
                        rotate(n, 1, S["swap_q"], S["rot_sin_q"], S["rot_cos_q"], S["rot_q"])
                        twice_silu(S["tanh_v"], n, yv, orr, yv, S["y_v"])
                    if s == 12:
                        e.wait_ge(S["sqk_ready"], n + 1)
                        e.tensor_reduce(ssk, by_sub(sqk), AX.X, ALU.add).then_inc(S["ss_steps"], 1)
                        e.wait_ge(S["sqq_ready"], n + 1)
                        e.tensor_reduce(ssq, by_sub(sqq), AX.X, ALU.add).then_inc(S["ss_steps"], 1)
                        e.wait_ge(S["ss_steps"], 3 * n + 2)
                        e.tensor_scalar(ss, ss, 4 * EPS, None, ALU.add).then_inc(S["ss_steps"], 1)
                    if s == 13:
                        e.wait_ge(S["nk_ready"], n + 1)
                        e.tensor_tensor(by_sub(knat), by_sub(bE), over_tokens(nk), ALU.mult).then_inc(S["k_nat"], 1)
                        e.wait_ge(S["s_out"], n + 1)
                        e.tensor_tensor(by_sub(rs[:, 2, :]), by_sub(bA), over_subs(cur[:, PAR_MASK:PAR]),
                                        ALU.mult).then_inc(S["s_masked"], 1)
                    if s == 14:
                        twice_silu(S["tanh_rg"], n, gts[:, 0, :], gts[:, 0, :], pr[:, RG - RK, :], S["y_rg"])
                        twice_silu(S["tanh_gz"], n, gts[:, 1, :], gts[:, 1, :], pr[:, GZ - RK, :], S["y_gz"])
                    if s == 17:
                        e.wait_ge(S["kk_out"], n + 1)
                        e.wait_ge(S["beta_d"], n + 1)
                        e.tensor_tensor(LT, bB, bD, ALU.mult).then_inc(S["lt_ready"], 1)
                    if s in (16, 20, 24):
                        t = (s - 16) // 4
                        e.wait_ge(S["r_cross"], SUB * n + t + 1)
                        e.wait_ge(S["r_upd"], n + 1)
                        if t:
                            e.wait_ge(S["r_state"], 3 * n + t)
                        e.scalar_tensor_tensor(out=Sr[:, :], in0=Sr[:, :], scalar=cur[:, C_SDEC:C_SDEC + 1],
                                               in1=sub(bA, t), op0=ALU.mult, op1=ALU.add).then_inc(S["r_state"], 1)
                    if s == 18:
                        e.wait_ge(S["lvl_mask"], LEVELS * n + 1)
                        e.tensor_tensor(by_sub(U), over_subs(ident), by_sub(Lm), ALU.subtract).then_inc(S["u_first"], 1)
                        e.tensor_tensor(attn, bF, Dm, ALU.mult).then_inc(S["attn_ready"], 1)
                    if 24 <= s <= 44 and s % 4 == 0:
                        l = (s - 24) // 4 + 1
                        e.wait_ge(S["y_out"], (LEVELS - 1) * n + l)
                        if l < LEVELS - 1:
                            if l > 1:
                                e.wait_ge(S["t_next"], (LEVELS - 2) * n + l - 1)
                            else:
                                e.wait_ge(S["t_ready"], n + 1)
                            e.tensor_tensor(T, T, bB, ALU.subtract).then_inc(S["t_next"], 1)
                        if l > 1:
                            e.wait_ge(S["u_next"], (LEVELS - 1) * n + l - 1)
                        e.tensor_tensor(U, U, bF, ALU.subtract).then_inc(S["u_next"], 1)
                    if s == 28:
                        e.wait_ge(S["r_cross"], SUB * n + SUB)
                        e.wait_ge(S["r_state"], 3 * n + 3)
                        e.scalar_tensor_tensor(out=Sr[:, :], in0=Sr[:, :], scalar=cur[:, C_SDEC:C_SDEC + 1],
                                               in1=sub(bA, SUB - 1), op0=ALU.mult, op1=ALU.add).then_inc(S["state_kept"], 1)
                        e.tensor_scalar(orr, bC, cur[:, C_QDEC:C_QDEC + 1], None, ALU.mult).then_inc(S["ro_steps"], 1)
                        e.wait_ge(S["ro_steps"], 6 * n + 1)
                        e.tensor_tensor(orr, orr, bD_, ALU.add).then_inc(S["ro_steps"], 1)
                        e.wait_ge(S["ro_steps"], 6 * n + 2)
                        e.tensor_reduce(rme, by_sub(orr), AX.X, ALU.add).then_inc(S["ro_steps"], 1)
                        e.wait_ge(S["ro_steps"], 6 * n + 3)
                        e.scalar_tensor_tensor(out=by_sub(orr), in0=over_tokens(rme), scalar=-1.0 / P, in1=by_sub(orr),
                                               op0=ALU.mult, op1=ALU.add).then_inc(S["ro_steps"], 1)
                        e.wait_ge(S["state_kept"], 2 * n + 1)
                        e.tensor_scalar(states[:, 0, u, :], Sr[:, :], one, None, ALU.mult).then_inc(S["sr_kept"], 1)
                    if s == 32:
                        e.wait_ge(S["rsq"], n + 1)
                        e.tensor_reduce(rva, by_sub(th), AX.X, ALU.add).then_inc(S["rvar"], 1)
                        e.wait_ge(S["rvar"], n + 1)
                        e.tensor_scalar(rva, rva, 4.0 / P, 4 * EPS, ALU.mult, ALU.add).then_inc(S["ro_steps"], 1)
                    if s == 34:
                        e.wait_ge(S["rpow"], n + 1)
                        e.tensor_tensor(by_sub(orr), by_sub(orr), over_tokens(rrs), ALU.mult).then_inc(S["ro_steps"], 1)
                    if s == 36:
                        e.wait_ge(S["ro_t"], n + 1)
                        e.wait_ge(S["w_used"], 8 * quarter_of(b, 0))
                        mixed(n, S["mix_r"], bC, cur[:, C_RETW:C_RETW + 1], gts[:, 0, :], orr, lambda h: mT[:, h, u, :])
                    if s in range(46, 62, 4):
                        t = (s - 46) // 4
                        e.wait_ge(S["ks_out"], SUB * n + t + 1)
                        if t == 0:
                            e.wait_ge(S["negc_ready"], n + 1)
                        else:
                            e.wait_ge(S["tr_out"], SUB * n + t)
                        e.scalar_tensor_tensor(out=rv_[:, 0, :], in0=sub(bB, t), scalar=negc[:, t:t + 1],
                                               in1=sub(vnat, t), op0=ALU.mult, op1=ALU.add).then_inc(S["r_ready"], 1)
                    if s in range(49, 65, 4):
                        t = (s - 49) // 4
                        e.wait_ge(S["upd_out"], SUB * n + t + 1)
                        if t:
                            e.wait_ge(S["g_state"], SUB * n + t)
                        e.scalar_tensor_tensor(out=Sg[:, :], in0=Sg[:, :], scalar=eg[:, 8 + t:9 + t],
                                               in1=sub(bD_, t), op0=ALU.mult, op1=ALU.add).then_inc(S["g_state"], 1)
                e.wait_ge(S["o2_out"], SUB * n + SUB)
                e.tensor_tensor(by_sub(og), by_sub(bF), over_tokens(eg[:, 0:4]), ALU.mult).then_inc(S["go_steps"], 1)
                e.wait_ge(S["go_steps"], 6 * n + 1)
                e.tensor_tensor(og, og, bA, ALU.add).then_inc(S["go_steps"], 1)
                e.tensor_tensor(gtm, nq, nq, ALU.mult).then_inc(S["gfac"], 1)
                e.wait_ge(S["g_state"], SUB * n + SUB)
                e.tensor_scalar(states[:, 1, u, :], Sg[:, :], one, None, ALU.mult).then_inc(S["state_kept"], 1)
                e.wait_ge(S["gsq"], n + 1)
                e.tensor_reduce(gva, by_sub(sqk), AX.X, ALU.add).then_inc(S["go_steps"], 1)
                e.wait_ge(S["gfac"], n + 1)
                e.wait_ge(S["go_steps"], 6 * n + 3)
                e.tensor_tensor(gtm, gtm, gva, ALU.mult).then_inc(S["go_steps"], 1)
                e.wait_ge(S["go_steps"], 6 * n + 4)
                e.tensor_scalar(gtm, gtm, 4.0 / (P * DK), 4 * EPS, ALU.mult, ALU.add).then_inc(S["gvar"], 1)
                e.wait_ge(S["gpow"], n + 1)
                e.scalar_tensor_tensor(out=gfa, in0=nq, scalar=float(DK) ** -0.5, in1=grs, op0=ALU.mult,
                                       op1=ALU.mult).then_inc(S["go_steps"], 1)
                e.wait_ge(S["go_steps"], 6 * n + 5)
                e.tensor_tensor(by_sub(og), by_sub(og), over_tokens(gfa), ALU.mult).then_inc(S["go_steps"], 1)
                e.wait_ge(S["go_t"], n + 1)
                mixed(n, S["mix_g"], bE, cur[:, C_GDNW:C_GDNW + 1], gts[:, 1, :], og, lambda h: mT[:, h, HEADS + u, :])

            e.memset(mhalf, -0.5).then_inc(S["host_consts"], 1)
            e.memset(states[:, :, :, :], 0.0).then_inc(S["host_consts"], 1)
            e.memset(hist[:, :, :], 0.0).then_inc(S["host_consts"], 1)
            e.wait_ge(S["silu_c"], 2)
            e.wait_ge(S["mod_par_in"], 64)
            e.tensor_scalar(negA, negA, -1.0, None, ALU.mult).then_inc(S["silu_v"], 1)
            e.tensor_scalar(scol, scol, one, None, ALU.add).then_inc(S["silu_v"], 1)
            e.wait_ge(S["silu_v"], 2)
            e.reciprocal(scol, scol).then_inc(S["silu_v"], 1)
            e.wait_ge(S["silu_v"], 3)
            e.tensor_tensor(scol, scol, ccol, ALU.mult).then_inc(S["silu_v"], 1)
            e.wait_ge(S["silu_v"], 4)
            def ada_sum(g):
                for j in range(KT):
                    k = KT * g + j
                    e.wait_ge(ADASEM[ada_at[k]], 16 * (ada_turn[k] + 1))
                    if j == 0:
                        ins = e.tensor_scalar(ada_acc[g], ada_slot(k), scol[:, 0:1], None, ALU.mult)
                    else:
                        e.wait_ge(S["ada_sums"], k)
                        ins = e.scalar_tensor_tensor(out=ada_acc[g], in0=ada_slot(k), scalar=scol[:, j:j + 1],
                                                     in1=ada_acc[g], op0=ALU.mult, op1=ALU.add)
                    ins.then_inc(S["ada_sums"], 1)

            ada_sum(0)
            e.wait_ge(S["mod_cols"], 1)
            e.tensor_tensor(mod[:, 0:16], bC[:, 0:32:2], adab[:, 0:16], ALU.add).then_inc(S["mod_steps"], 1)
            e.wait_ge(S["mod_steps"], 1)
            e.tensor_copy(B1, mod[:, 0:8]).then_inc(S["mod_steps"], 1)
            e.scalar_tensor_tensor(out=A1, in0=mod[:, 8:16], scalar=one, in1=nrm[:, 0:8], op0=ALU.add,
                                   op1=ALU.mult).then_inc(S["mod_steps"], 1)
            e.wait_ge(S["mod_steps"], 3)
            e.wait_ge(S["host_consts"], 3)
            e.wait_ge(S["wg_split"], 1)
            e.tensor_tensor(wgs[:, 1, :, :], wg[:, :, :], wgs[:, 0, :, :].bitcast(F32), ALU.subtract).then_inc(S["wg_split"], 1)
            e.sem_inc(S["mod_ready"], 1)
            e.wait_ge(S["x1_in"], 16)
            for j in range(1, KT):
                add_square(0, j)
            row_of(0)
            normed(0, 0, bA)
            e.wait_ge(S["xn_ready"], KT)
            gates(0)
            ada_sum(1)
            ada_sum(2)
            e.wait_ge(S["mod_cols"], 3)
            e.tensor_tensor(mod[:, 16:48], bC[:, 32:96:2], adab[:, 16:48], ALU.add).then_inc(S["mod_steps"], 1)
            e.wait_ge(S["mod_steps"], 4)
            e.tensor_copy(GA, mod[:, 16:24]).then_inc(S["mod_steps"], 1)
            e.tensor_copy(B2, mod[:, 24:32]).then_inc(S["mod_steps"], 1)
            e.tensor_copy(GM, mod[:, 40:48]).then_inc(S["mod_steps"], 1)
            e.tensor_copy(WF, nrm[:, 16:24]).then_inc(S["mod_steps"], 1)
            e.scalar_tensor_tensor(out=A2, in0=mod[:, 32:40], scalar=one, in1=nrm[:, 8:16], op0=ALU.add,
                                   op1=ALU.mult).then_inc(S["mod_steps"], 1)
            e.wait_ge(S["mod_steps"], 9)
            e.sem_inc(S["mod_ready"], 1)

            with e.Fori(0, NB) as b:
                with e.Fori(0, HEADS - 2) as u:
                    unit_start(b, u, b * HEADS + u)
                    unit(b, u, b * HEADS + u)
                for j in range(1, KT):
                    add_square(norm_no(b, 0), j)
                row_of(norm_no(b, 0))
                e.tensor_copy(row1[:, :], bA).then_inc(S["row_kept"], 1)
                unit_start(b, HEADS - 2, b * HEADS + HEADS - 2)
                unit(b, HEADS - 2, b * HEADS + HEADS - 2)
                unit_start(b, HEADS - 1, b * HEADS + HEADS - 1)
                e.wait_ge(S["row_kept"], b + 1)
                normed(norm_no(b, 0), 1 + 2 * b, row1[:, :])
                unit(b, HEADS - 1, b * HEADS + HEADS - 1)
                gates(b + 1)
                e.wait_ge(S["x1_in"], 48 + 32 * b)
                for j in range(KT):
                    e.wait_ge(S["w_used"], 8 * quarter_of(b, OUT0) + 2 * j + 2)
                    e.scalar_tensor_tensor(out=x1[:, j, :], in0=acc[:, j % 2, :], scalar=GA[:, j:j + 1],
                                           in1=x1[:, j, :], op0=ALU.mult, op1=ALU.add).then_inc(S["out_evac"], 1)
                    if j >= 2:
                        add_square(norm_no(b, 1), j - 1)
                add_square(norm_no(b, 1), KT - 1)
                row_of(norm_no(b, 1))
                normed(norm_no(b, 1), 2 + 2 * b, bA)

                def ff1(g):
                    for i in range(FFG):
                        f = NG * FFG * b + FFG * g + i
                        e.wait_ge(S["ff1_relu"], f + 1)
                        e.wait_ge(S["hid_lo"], f - 1 if i >= 2 else NG * FFG * b + FFG * g)
                        e.scalar_tensor_tensor(out=io[:, 2 + i % 2, :], in0=acc[:, i % 2, :], scalar=0.0,
                                               in1=io[:, i % 2, :], op0=ALU.max, op1=ALU.mult).then_inc(S["ff1_evac"], 1)

                def ff2(q, g, squares=False):
                    for o in range(2 * FFG):
                        f = 2 * NG * FFG * b + 2 * FFG * g + o
                        e.wait_ge(S["w_used"], 8 * q + o + 1)
                        e.wait_ge(S["ff2_evac"], f)
                        e.scalar_tensor_tensor(out=x1[:, o, :], in0=acc[:, o % 2, :], scalar=GM[:, o:o + 1],
                                               in1=x1[:, o, :], op0=ALU.mult, op1=ALU.add).then_inc(S["ff2_evac"], 1)
                        if squares and o >= 2:
                            add_square(norm_no(b, 2), o - 1, sqrow_last)

                ffq = quarter_of(b, FF0)
                ff1(0)
                ff1(1)
                ff2(ffq + 2, 0)
                with e.Fori(0, ff_pairs) as r:
                    ff1(2 * r + 2)
                    ff2(ffq + 4 + 4 * r, 2 * r + 1)
                    ff1(2 * r + 3)
                    ff2(ffq + 6 + 4 * r, 2 * r + 2)
                ff2(ffq + 2 * NG - 1, NG - 1, squares=True)
                add_square(norm_no(b, 2), KT - 1, sqrow_last)
                row_of(norm_no(b, 2))
                e.wait_ge(S["sq_added"], (KT - 1) * (norm_no(b, 2) + 1))
                for j in range(KT):
                    if j >= 4:
                        e.wait_ge(OSEM[j % 4], 16 * (2 * b + 1))
                    e.scalar_tensor_tensor(out=io[:, j % 4, :], in0=x1[:, j, :], scalar=WF[:, j:j + 1], in1=bA,
                                           op0=ALU.mult, op1=ALU.mult).then_inc(S["o_ready"], 1)

        @block.gpsimd
        def _(e):
            def lo(q, local):
                tile = local // 2
                e.wait_ge(S["w_hi"], 8 * q + local + 1)
                e.tensor_tensor(w2[:, 1, local % HALVES, :], raw[:, tile % NRAW, local % 2 * NT:(local % 2 + 1) * NT],
                                w2[:, 0, local % HALVES, :].bitcast(F32), ALU.subtract).then_inc(S["w_lo"], 1)

            def rms_power(n):
                e.wait_ge(S["ms_ready"], n + 1)
                e.tensor_tensor(rstd, ms, mhalf[:, 0:4], ALU.pow).then_inc(S["rstd_ready"], 1)

            def low_parts(hn, dst):
                for j in range(KT):
                    e.wait_ge(S["h_hi"], KT * hn + j + 1)
                    e.tensor_tensor(dst[:, 1, j, :], io[:, 2 + j % 2, :], dst[:, 0, j, :].bitcast(F32),
                                    ALU.subtract).then_inc(S["h_lo"], 1)

            def unit(b, n, q):
                e.wait_ge(S["w_used"], 8 * quarter_of(b, 0))
                for s in range(UNIT * KT):
                    if s % 4 == 0:
                        lo(q, s // 4 + 3)
                    if s == 0:
                        e.wait_ge(S["unit_start"], 6 * n + 6)
                        e.tensor_tensor(by_sub(gs), over_subs(strict), over_tokens(cgb[:, 0:SUB]), ALU.mult).then_inc(S["gstrict"], 1)
                        e.wait_ge(S["cs_in"], 32 + 32 * b)
                        e.tensor_tensor(rot[:, 0, :], pr[:, 0, :], cs[:, 0, :], ALU.mult).then_inc(S["rot_cos_k"], 1)
                    if s == 2:
                        e.tensor_tensor(rot[:, 1, :], pr[:, 1, :], cs[:, 0, :], ALU.mult).then_inc(S["rot_cos_q"], 1)
                    if s == 5:
                        e.wait_ge(S["d_exp"], n + 1)
                        e.tensor_tensor(by_sub(Dm), by_sub(Dm), over_subs(upper), ALU.mult).then_inc(S["d_mask"], 1)
                    if s == 7:
                        e.wait_ge(S["d_mask"], n + 1)
                        e.tensor_tensor(by_sub(bD), by_sub(Dm), over_tokens(cgb[:, SUB:2 * SUB]), ALU.mult).then_inc(S["beta_d"], 1)
                    if s == 12:
                        e.wait_ge(S["ss_steps"], 3 * n + 3)
                        e.tensor_tensor(nkq, ss, mhalf, ALU.pow).then_inc(S["nk_ready"], 1)
                    if s == 17:
                        e.wait_ge(S["lt_ready"], n + 1)
                        e.tensor_tensor(by_sub(Lm), by_sub(LT), over_subs(lmask[:, 0, :]), ALU.mult).then_inc(S["lvl_mask"], 1)
                    if 18 <= s <= 38 and s % 4 == 2:
                        l = (s - 18) // 4 + 1
                        if l == 1:
                            e.wait_ge(S["u_first"], n + 1)
                        else:
                            e.wait_ge(S["x_out"], (LEVELS - 1) * n + l - 1)
                        e.tensor_tensor(by_sub(Lm), by_sub(LT), over_subs(lmask[:, l, :]), ALU.mult).then_inc(S["lvl_mask"], 1)
                    if s == 33:
                        e.wait_ge(S["ro_steps"], 6 * n + 5)
                        e.tensor_tensor(rrs, rva, mhalf[:, 0:4], ALU.pow).then_inc(S["rpow"], 1)
                    if s == 41:
                        e.wait_ge(S["kt_out"], n + 1)
                        e.wait_ge(S["gc_exp"], n + 1)
                        e.tensor_tensor(by_sub(knat), by_sub(knat), over_tokens(eg[:, 4:8]), ALU.mult).then_inc(S["kd_ready"], 1)
                e.wait_ge(S["gvar"], n + 1)
                e.tensor_tensor(grs, gtm, mhalf[:, 0:4], ALU.pow).then_inc(S["gpow"], 1)

            e.wait_ge(S["const_in"], 32)
            e.wait_ge(S["lmask_in"], 16)
            e.wait_ge(S["host_consts"], 3)
            for h in range(3):
                lo(0, h)
            rms_power(0)
            low_parts(0, hT)
            for i in range(UNIT):
                lo(0, 2 * i + 3)
                lo(0, 2 * i + 4)
            with e.Fori(0, NB) as b:
                with e.Fori(0, HEADS - 2) as u:
                    unit(b, b * HEADS + u, quarter_of(b, 0) + u * (UNIT // 4))
                rms_power(norm_no(b, 0))
                unit(b, b * HEADS + HEADS - 2, quarter_of(b, (HEADS - 2) * UNIT))
                low_parts(1 + 2 * b, hT)
                unit(b, b * HEADS + HEADS - 1, quarter_of(b, (HEADS - 1) * UNIT))
                for j in range(2 * KT):
                    lo(quarter_of(b, OUT0), j + 3)
                rms_power(norm_no(b, 1))
                low_parts(2 + 2 * b, mT)

                def ff1(q, g, par):
                    for i in range(FFG):
                        lo(q, 2 * i + 3)
                        lo(q, 2 * i + 4)
                        e.wait_ge(S["hid_hi"], NG * FFG * b + FFG * g + i + 1)
                        e.tensor_tensor(hid[:, par, 1, i, :], io[:, 2 + i % 2, :], hid[:, par, 0, i, :].bitcast(F32),
                                        ALU.subtract).then_inc(S["hid_lo"], 1)

                def ff2(q):
                    for i in range(2 * FFG):
                        lo(q, i + 3)

                ffq = quarter_of(b, FF0)
                ff1(ffq, 0, 0)
                ff1(ffq + 1, 1, 1)
                ff2(ffq + 2)
                with e.Fori(0, ff_pairs) as r:
                    ff1(ffq + 3 + 4 * r, 2 * r + 2, 0)
                    ff2(ffq + 4 + 4 * r)
                    ff1(ffq + 5 + 4 * r, 2 * r + 3, 1)
                    ff2(ffq + 6 + 4 * r)
                ff2(ffq + 2 * NG - 1)
                rms_power(norm_no(b, 2))


def constants():
    r = np.arange(P)
    f = np.float32
    masks = np.zeros((P, 4 + LEVELS, P), f)
    masks[:, 0] = np.eye(P)
    masks[:, 1] = 1.0
    masks[:, 2] = r[:, None] <= r[None, :]
    masks[:, 3] = r[:, None] > r[None, :]
    for l in range(LEVELS):
        m = 1 << l
        masks[:, 4 + l] = ((r[:, None] // (2 * m) == r[None, :] // (2 * m))
                           & (r[:, None] // m % 2 == 0) & (r[None, :] // m % 2 == 1))
    inv = (10000.0 ** (-np.arange(0, DK, 2, dtype=f) / f(DK))).astype(f)
    ang = (np.arange(SEQ, dtype=f)[:, None] * inv[None, :]).astype(f).astype(np.float64)
    cos, sin = np.cos(ang).T, np.sin(ang).T
    cos = np.concatenate([cos, cos]).astype(f).reshape(P, NB, NT).transpose(1, 0, 2)
    sin = np.concatenate([-sin, sin]).astype(f).reshape(P, NB, NT).transpose(1, 0, 2)
    par = np.zeros((P, HEADS, PAR), f)
    s, c = r[:, None], r[None, :]
    for h in range(HEADS):
        lg = np.log(1.0 - 2.0 ** (-5.0 - h))
        scale = DK ** -0.5
        par[:, h, C_QDEC] = np.exp(lg * (r + 1))
        par[:, h, C_KDEC] = np.exp(lg * (P - 1 - r)) * scale
        par[:, h, C_SDEC] = np.exp(lg * P)
        seen = (s // CHUNK) <= (c // CHUNK)
        par[:, h, PAR_MASK:] = np.where(seen, np.exp(lg * np.abs(c - s)), 0.0) * scale
    return masks, np.ascontiguousarray(cos), np.ascontiguousarray(sin), par


def layout(x, c, ada_w, ada_b, norm_mix_w, w_in, conv_w, a_log, dt_bias, ret_norm_w, gdn_norm_w, w_out,
           norm_mlp_w, w_ff1, w_ff2, norm_final_w):
    masks, cos, sin, par = constants()

    def cols(v):
        return v.reshape(-1, P).T

    def tile(w):
        return w.reshape(KT, P, P).transpose(1, 0, 2).reshape(P, KT * P)

    w_in, w_out, w1, w2 = w_in[0], w_out[0], w_ff1[0], w_ff2[0]
    first = {RQ: 0, RK: 512, RV: 1024, RG: 1536, GQ: 2048, GK: 2560, GV: 3072, GZ: 3584}
    stream = []
    for u in (1, 2, 3, 0):
        for i in range(UNIT):
            at = first[i] + u * P
            stream.append(tile(w_in[:, at:at + P]))
    for j in range(KT):
        stream.append(tile(w_out[:, j * P:(j + 1) * P]))

    def ff1(g):
        for i in range(FFG):
            at = (g * FFG + i) * P
            stream.append(tile(w1[:, at:at + P]))

    def ff2(g):
        rows = w2[g * FFG * P:(g + 1) * FFG * P].reshape(FFG, P, KT, P)
        for i in range(FFG):
            part = rows[:, :, 2 * i:2 * i + 2, :]
            stream.append(part.transpose(1, 2, 0, 3).reshape(P, KT * P))

    ff1(0)
    for g in range(1, NG):
        ff1(g)
        ff2(g - 1)
    ff2(NG - 1)
    assert len(stream) == TILES_PER_BLOCK

    conv = conv_w[0].reshape(TAPS, 3, HEADS, P)
    for h in range(HEADS):
        for slot, which in ((GK, 1), (GQ, 0), (GV, 2)):
            par[:, h, 4 * slot:4 * slot + 4] = conv[:, which, h, :].T
        par[:, h, C_RETW] = ret_norm_w[0, h * P:(h + 1) * P]
        par[:, h, C_GDNW] = gdn_norm_w[0]
    return {
        "xT": x[0].reshape(NB, NT, KT, P).transpose(0, 3, 2, 1),
        "w_all": np.stack(stream),
        "w_gate": w_in[:, 4096:4104].reshape(KT, P, 8).transpose(1, 0, 2),
        "ada_w": ada_w[0].reshape(KT, P, 3, 2048).transpose(2, 0, 1, 3),
        "c_col": cols(c[0]),
        "ada_b": cols(ada_b[0]),
        "norms": np.concatenate([cols(norm_mix_w[0]), cols(norm_mlp_w[0]), cols(norm_final_w)], axis=1),
        "par": par,
        "masks": masks,
        "cos": cos,
        "sin": sin,
        "gate_par": np.broadcast_to(np.concatenate([a_log[0], dt_bias[0]])[None, :], (P, 8)),
    }


def kernel(**inputs):
    import concourse.bacc as bacc
    from concourse.bass_utils import run_bass_kernel_spmd

    nc = bacc.Bacc("TRN2", target_bir_lowering=False, num_devices=1)
    laid = layout(**{k: np.asarray(v) for k, v in inputs.items()})
    arrays, args = {}, []
    for name, a in laid.items():
        a = np.ascontiguousarray(a)
        arrays[f"in_{name}"] = a
        args.append(nc.dram_tensor(f"in_{name}", a.shape, mybir.dt.from_np(a.dtype), kind="ExternalInput").ap())
    out = nc.dram_tensor("out_0", (NB, P, KT, NT), F32, kind="ExternalOutput").ap()
    build(nc, *args, out)
    r = run_bass_kernel_spmd(nc, [arrays], core_ids=[0])
    o = r.results[0]["out_0"]
    return np.ascontiguousarray(o.transpose(0, 3, 2, 1).reshape(1, SEQ, D))
```

```python
from contextlib import ExitStack

import numpy as np

import concourse.bass as bass
from concourse import mybir

ACT = mybir.ActivationFunctionType
ALU = mybir.AluOpType
AX = mybir.AxisListType
F32 = mybir.dt.float32
F32R = mybir.dt.float32r

P = 128
D = 1024
SEQ = 2048
NT = 512
NB = SEQ // NT
KT = D // P
HEADS = 4
SUB = NT // P
CHUNK = 64
FF = 4 * D
EPS = 1e-6
DK = 128
TAPS = 4
HIST = TAPS - 1
UNIT = 8
GK, GQ, GV, RK, RQ, RV, RG, GZ = range(UNIT)
FFG = 4
NG = FF // P // FFG
TILES_PER_BLOCK = HEADS * UNIT + KT + NG * 2 * FFG
NRAW = 2
HALVES = 4
LEVELS = 7
PAR_MASK = 32
PAR = PAR_MASK + P
(C_RETW, C_GDNW, C_QDEC, C_KDEC, C_SDEC) = range(12, 17)

SEMAPHORES = """
const_in lmask_in cs_in par_in mod_par_in host_consts
raw0 raw1 w_hi w_lo w_used
ada0 ada1 ada2 ada3 silu_c ada_sums mod_cols mod_ready
sq_ready sq_added colsum_ready ms_ready rstd_ready diag_ready row_ready row_kept xn_ready
hf_ready h_hi h_lo
first_mask t_turned u_turned nq_ready
wg_split gate_rows gate_copied gate_out gate_steps gate_exp
proj_evac out_evac ff1_relu ff1_evac hid_hi hid_lo ff2_evac
unit_start front_start conv_steps tanh_k tanh_q tanh_v tanh_rg tanh_gz y_k y_q y_v y_rg y_gz
swap_k swap_q rot_cos_k rot_sin_k rot_cos_q rot_sin_q rot_k rot_q
gstrict d_out gc_out d_exp gc_exp d_mask beta_d
rt_out kdec_r v_r s_out s_masked r_upd r_cross r_state
gt_out sqk_ready sqq_ready ss_steps nk_ready k_nat kt_out kt_ready v_nat
kk_out attn_ready lt_ready lvl_mask u_first t_first_out t_ready x_out x_ready y_out t_next u_next
negc_ready gfac gvar rvar sr_kept silu_v mod_steps gates_done kd_ready ks_out r_ready tr_out vnew_ready upd_out g_state o2_out
ro_steps rsq rpow ro_t go_steps gsq gpow go_t
mix_r mix_g state_kept
o_ready o_dma0 o_dma1 o_dma2 o_dma3 x1_in
""".split()


def build(nc, xT, w_all, w_gate, ada_w, c_col, ada_b, norms, par, masks, cos, sin, gate_par, out):
    ctx = ExitStack()
    with ctx:
        def sb(name, shape, dt=F32):
            return ctx.enter_context(nc.sbuf_tensor(name, shape, dt))

        S = {n: ctx.enter_context(nc.semaphore(n)) for n in SEMAPHORES}

        hT = sb("hT", [P, 2, KT, NT], F32R)
        mT = sb("mT", [P, 2, KT, NT], F32R)
        w2 = sb("w2", [P, 2, HALVES, 4 * P], F32R)
        raw = sb("raw", [P, NRAW, KT * P])
        x1 = sb("x1", [P, KT, NT])
        hidden_ctx = nc.sbuf_tensor("hid", [P, 2, 2, FFG, NT], F32R)
        hid = hidden_ctx.__enter__()
        hidden_ctx.__exit__(None, None, None)
        mixing = sb("mixing", [P, 16, NT])
        (yk, sqk, sqq, gs, LT, orr, th, swp,
         yq, yv, knat, kT, vnat, Dm, attn, og) = (mixing[:, i, :] for i in range(16))
        T, U, X, Lm, bD = yk, yv, sqk, sqq, gs
        conv_at = {GK: yk, GQ: LT, GV: orr}
        tanh_at = {GK: th, GQ: sqk, GV: sqq}
        pg = sb("pg", [P, 3, HIST + NT])
        pr = sb("pr", [P, 5, NT])
        gts = sb("gts", [P, 2, NT])
        rot = sb("rot", [P, 2, NT])
        rs = sb("rs", [P, 3, NT])
        io = sb("io", [P, 4, NT])
        row1 = sb("row1", [P, NT])
        cs = sb("cs", [P, 2, NT])
        consts = sb("consts", [P, 4, P])
        lmask = sb("lmask", [P, LEVELS, P])
        para = sb("para", [P, HEADS, PAR])
        cur = sb("cur", [P, PAR])
        gb = sb("gb", [P, HEADS, 2 * SUB])
        cgb = sb("cgb", [P, 2 * SUB])
        cw = sb("cw", [P, 3 * TAPS])
        states = sb("states", [P, 2, HEADS, P])
        Sr = sb("Sr", [P, P])[:, :]
        Sg = sb("Sg", [P, P])[:, :]
        hist = sb("hist", [P, HEADS, 3 * HIST])
        rv_ = sb("rvv", [P, 2, P])
        small = sb("small", [P, 256])
        ab = sb("ab", [P, 48 + 7 * KT + 8 + 48])
        wg = sb("wg", [P, KT, 8])
        wgs = sb("wgs", [P, 2, KT, 8], F32R)

        ident, ones, upper, strict = (consts[:, i, :] for i in range(4))
        mod = ab[:, 0:48]
        A1, B1, GA, A2, B2, GM, WF = (ab[:, 48 + i * KT:48 + (i + 1) * KT] for i in range(7))
        ccol = ab[:, 104:112]
        adab = ab[:, 112:160]
        nrm = small[:, 0:24]
        gpar = small[:, 24:32]
        mhalf = small[:, 240:248]
        ms, rstd = small[:, 36:40], small[:, 40:44]
        negA = small[:, 44:48]
        eg = small[:, 48:60]
        negc = small[:, 60:64]
        ssk, ssq, nk, nq = (small[:, 64 + 4 * i:68 + 4 * i] for i in range(4))
        rme, rva, rrs = (small[:, 80 + 4 * i:84 + 4 * i] for i in range(3))
        gva, grs, gfa, gtm = (small[:, 92 + 4 * i:96 + 4 * i] for i in range(4))
        gx, gu, gz_, gp, gq_ = (small[:, 112 + 16 * i:128 + 16 * i] for i in range(5))
        gbt = small[:, 192:208]
        scol = small[:, 208:216]
        stmp = small[:, 216:224]

        acc = ctx.enter_context(nc.psum_tensor("acc", [P, 2, 512], F32))
        pm = ctx.enter_context(nc.psum_tensor("pm", [P, 6, 512], F32))
        bA, bB, bC, bD_, bE, bF = (pm[:, i, :] for i in range(6))

        block = ctx.enter_context(nc.Block())

        def sub(ap, t):
            return ap[:, t * P:(t + 1) * P]

        def by_sub(ap):
            return ap.rearrange("p (t c) -> p t c", t=SUB)

        def over_tokens(col4):
            return col4.unsqueeze(2).to_broadcast([P, SUB, P])

        def over_subs(m):
            return m.unsqueeze(1).to_broadcast([P, SUB, P])

        sqrow, dg = row1[:, :], io[:, 2, :]
        gateT = io[:, 3, :]

        def tile_of(b, phase_tile):
            return UNIT + TILES_PER_BLOCK * b + phase_tile

        def proj_of(b, u):
            return UNIT + HEADS * UNIT * b + UNIT * u

        OUT0 = HEADS * UNIT
        FF0 = OUT0 + KT

        def out_quarter(b, last):
            return quarter_of(b, OUT0) - (UNIT // 4 if last else 0)

        def proj_end(b, last):
            return proj_of(b, HEADS) - (UNIT if last else 0)

        LEAD = KT

        def norm_no(b, which):
            return 1 + 3 * b + which

        RAWSEM = (S["raw0"], S["raw1"])
        ADASEM = (S["ada0"], S["ada1"], S["ada2"], S["ada3"])
        ada_at = [k % 4 for k in range(KT)] + [k % 3 for k in range(2 * KT)]
        ada_turn = [ada_at[:k].count(ada_at[k]) for k in range(3 * KT)]
        OSEM = (S["o_dma0"], S["o_dma1"], S["o_dma2"], S["o_dma3"])
        GSTEPS = 19
        ff_pairs = NG // 2 - 1

        def quarter_of(b, t):
            return (UNIT + t) // 4 + (TILES_PER_BLOCK // 4) * b

        def ada_slot(k):
            at = 4 * ada_at[k]
            return mixing[:, at:at + 4, :].rearrange("p a n -> p (a n)")

        ada_acc = [x.rearrange("p a n -> p (a n)") for x in (io[:, :, :], x1[:, 0:4, :], x1[:, 4:8, :])]

        @block.sync
        def _(e):
            e.dma_start(ab[:, 104:112], c_col).then_inc(S["mod_par_in"], 16)
            e.dma_start(ab[:, 112:160], ada_b).then_inc(S["mod_par_in"], 16)
            e.dma_start(nrm, norms).then_inc(S["mod_par_in"], 16)
            e.dma_start(gpar, gate_par).then_inc(S["mod_par_in"], 16)
            e.dma_start(consts[:, :, :], masks[:, 0:4, :]).then_inc(S["const_in"], 16)
            e.dma_start(wg[:, :, :], w_gate).then_inc(S["const_in"], 16)
            def load(q, i, index, wait=True):
                if wait:
                    e.wait_ge(S["w_lo"], 8 * q + 2 * (i - NRAW) + 2)
                e.dma_start(raw[:, i % NRAW, :], w_all[index]).then_inc(RAWSEM[i % NRAW], 16)

            for k in range(3 * KT):
                if ada_turn[k]:
                    before = max(j for j in range(k) if ada_at[j] == ada_at[k])
                    e.wait_ge(S["ada_sums"], before + 1)
                e.dma_start(ada_slot(k), ada_w[k // KT, k % KT]).then_inc(ADASEM[ada_at[k]], 16)
                if k == 3:
                    load(0, 0, (HEADS - 1) * UNIT, wait=False)
                    load(0, 1, (HEADS - 1) * UNIT + 1, wait=False)
                    e.dma_start(x1[:, :, :], xT[0]).then_inc(S["x1_in"], 16)
                    e.dma_start(lmask[:, :, :], masks[:, 4:4 + LEVELS, :]).then_inc(S["lmask_in"], 16)
                    e.dma_start(para[:, :, :], par).then_inc(S["par_in"], 16)
                    e.dma_start(cs[:, 0, :], cos[0]).then_inc(S["cs_in"], 16)
                    e.dma_start(cs[:, 1, :], sin[0]).then_inc(S["cs_in"], 16)
                if k in (10, 13, 16, 19):
                    i = 2 + (k - 10) // 3
                    load(i // 4, i % 4, (HEADS - 1) * UNIT + i)

            for i in range(6, UNIT):
                load(i // 4, i % 4, (HEADS - 1) * UNIT + i)
            with e.Fori(0, NB - 1) as b:
                with e.Fori(0, TILES_PER_BLOCK // 4) as q:
                    for i in range(4):
                        load(quarter_of(b, 0) + q, i, q * 4 + i)
            with e.Fori(0, (HEADS - 1) * UNIT // 4) as q:
                for i in range(4):
                    load(quarter_of(NB - 1, 0) + q, i, q * 4 + i)
            with e.Fori(0, (TILES_PER_BLOCK - OUT0) // 4) as q:
                for i in range(4):
                    load(out_quarter(NB - 1, True) + q, i, q * 4 + OUT0 + i)
            for i in range(2):
                load(quarter_of(NB, 0) - UNIT // 4, i, i)

        @block.tensor
        def _(e):
            def step(q, i, half, k, x, bank, first, last):
                local = 2 * i + half
                if k == 0:
                    e.wait_ge(S["w_lo"], 8 * q + local + 1)
                slot = local % HALVES
                whi = w2[:, 0, slot, k * P:(k + 1) * P]
                wlo = w2[:, 1, slot, k * P:(k + 1) * P]
                e.matmul(bank, whi, x[:, 0, :], start=first, stop=False)
                e.matmul(bank, whi, x[:, 1, :], start=False, stop=False)
                m = e.matmul(bank, wlo, x[:, 0, :], start=False, stop=last)
                return m.then_inc(S["w_used"], 1) if k == 3 else m

            def column_sums(n, bank):
                e.wait_ge(S["sq_added"], (KT - 1) * (n + 1))
                for t in range(SUB):
                    m = e.matmul(bank[:, 2 * t:2 * t + 2], sub(sqrow, t), ones[:, 0:2], start=True, stop=True)
                m.then_inc(S["colsum_ready"], 1)

            def row_everywhere(n, bank):
                e.wait_ge(S["diag_ready"], n + 1)
                e.matmul(bank, ones, dg, start=True, stop=True).then_inc(S["row_ready"], 1)

            def stats(n):
                column_sums(n, bB)
                row_everywhere(n, bA)

            def gate_rows(hn):
                e.wait_ge(S["h_lo"], KT * (hn + 1))
                for k in range(KT):
                    e.matmul(bF[0:8, :], wgs[:, 0, k, :], hT[:, 0, k, :], start=k == 0, stop=False)
                    e.matmul(bF[0:8, :], wgs[:, 1, k, :], hT[:, 0, k, :], start=False, stop=False)
                    m = e.matmul(bF[0:8, :], wgs[:, 0, k, :], hT[:, 1, k, :], start=False, stop=k == KT - 1)
                m.then_inc(S["gate_rows"], 1)

            def gate_columns(m):
                e.wait_ge(S["gate_copied"], m + 1)
                turn(bF, gateT).then_inc(S["gate_out"], 1)

            def four(bank, lhs, rhs):
                for t in range(SUB):
                    m = e.matmul(sub(bank, t), sub(lhs, t), sub(rhs, t), start=True, stop=True)
                return m

            def turn(bank, x):
                for t in range(SUB):
                    m = e.transpose(sub(bank, t), sub(x, t), ident)
                return m

            def project(q, pt, s, hn=None):
                i, k = s // KT, s % KT
                if k == 0:
                    e.wait_ge(S["proj_evac"], pt + i - 1)
                if hn is not None and i == 0:
                    e.wait_ge(S["h_lo"], KT * hn + k + 1)
                step(q + i // 4, i % 4, k // 4, k % 4, hT[:, :, k, :], acc[:, i % 2, :], k == 0, k == KT - 1)

            def mix(b, u, n, s):
                if s == 8:
                    e.wait_ge(S["row_kept"], 2 * b)
                    e.wait_ge(S["gstrict"], n + 1)
                    e.wait_ge(S["unit_start"], 4 * n + 1)
                    for t in range(SUB):
                        m = e.matmul(sub(bA, t), sub(gs, t), upper, start=True, stop=True)
                    m.then_inc(S["d_out"], 1)
                    for j, w in enumerate((upper, strict, ones)):
                        m = e.matmul(bB[:, 4 * j:4 * j + 4], w, cgb[:, 0:SUB], start=True, stop=True)
                    m.then_inc(S["gc_out"], 1)
                if s == 9:
                    e.wait_ge(S["rot_k"], n + 1)
                    e.wait_ge(S["mix_r"], 3 * n)
                    turn(bC, rot[:, 0, :])
                    turn(bD_, pr[:, RV - RK, :]).then_inc(S["rt_out"], 1)
                if s == 11:
                    e.wait_ge(S["y_k"], n + 1)
                    e.wait_ge(S["y_q"], n + 1)
                    e.wait_ge(S["y_v"], n + 1)
                    e.wait_ge(S["gc_exp"], n + 1)
                    e.wait_ge(S["mix_g"], 3 * n)
                    turn(bE, yk)
                    turn(bF, yq)
                    turn(bB, yv).then_inc(S["gt_out"], 1)
                if s == 13:
                    e.wait_ge(S["rot_q"], n + 1)
                    e.wait_ge(S["d_exp"], n + 1)
                    four(bA, rot[:, 0, :], rot[:, 1, :]).then_inc(S["s_out"], 1)
                if s == 15:
                    e.wait_ge(S["k_nat"], n + 1)
                    turn(bE, knat).then_inc(S["kt_out"], 1)
                if s == 16:
                    e.wait_ge(S["kdec_r"], n + 1)
                    e.wait_ge(S["v_r"], n + 1)
                    e.wait_ge(S["s_masked"], n + 1)
                    four(bA, rs[:, 0, :], rs[:, 1, :])
                    four(bD_, rs[:, 2, :], rs[:, 1, :]).then_inc(S["r_upd"], 1)
                if s in (16, 19, 23, 27):
                    t = (16, 19, 23, 27).index(s)
                    if t:
                        e.wait_ge(S["r_state"], 3 * n + t)
                    e.wait_ge(S["unit_start"], 4 * n + 2)
                    e.matmul(sub(bC, t), sub(rot[:, 1, :], t), Sr, start=True, stop=True).then_inc(S["r_cross"], 1)
                if s == 17:
                    e.wait_ge(S["kt_ready"], n + 1)
                    e.wait_ge(S["v_nat"], n + 1)
                    e.wait_ge(S["sqq_ready"], n + 1)
                    four(bB, kT, kT)
                    four(bF, kT, yq).then_inc(S["kk_out"], 1)
                if s == 20:
                    e.wait_ge(S["u_first"], n + 1)
                    turn(bE, U).then_inc(S["t_first_out"], 1)
                if 22 <= s <= 42 and s % 4 == 2:
                    l = (s - 22) // 4 + 1
                    e.wait_ge(S["lvl_mask"], (LEVELS - 1) * n + l)
                    if l == 1:
                        e.wait_ge(S["t_ready"], n + 1)
                    else:
                        e.wait_ge(S["t_next"], (LEVELS - 2) * n + l - 1)
                        turn(bF, T).then_inc(S["t_turned"], 1)
                    four(bE, Lm, T).then_inc(S["x_out"], 1)
                if 24 <= s <= 44 and s % 4 == 0:
                    l = (s - 24) // 4 + 1
                    e.wait_ge(S["x_ready"], (LEVELS - 1) * n + l)
                    if l > 1:
                        e.wait_ge(S["u_turned"], (LEVELS - 2) * n + l - 1)
                    else:
                        e.wait_ge(S["attn_ready"], n + 1)
                        e.wait_ge(S["lt_ready"], n + 1)
                    if l < LEVELS - 1:
                        four(bB, U, X).then_inc(S["y_out"], 1)
                    else:
                        four(bF, X, U).then_inc(S["y_out"], 1)
                if s == 36:
                    e.wait_ge(S["ro_steps"], 6 * n + 6)
                    turn(bC, orr).then_inc(S["ro_t"], 1)
                if s in range(46, 62, 4):
                    t = (s - 46) // 4
                    if t == 0:
                        e.wait_ge(S["u_next"], n + 1)
                    else:
                        e.wait_ge(S["g_state"], SUB * n + t)
                    e.matmul(sub(bB, t), sub(kT, t), Sg, start=True, stop=True).then_inc(S["ks_out"], 1)
                    e.matmul(sub(bF, t), sub(yq, t), Sg, start=True, stop=True)
                if s in range(47, 63, 4):
                    t = (s - 47) // 4
                    e.wait_ge(S["r_ready"], SUB * n + t + 1)
                    e.matmul(sub(bE, t), sub(U, t), rv_[:, 0, :], start=True, stop=True).then_inc(S["tr_out"], 1)
                if s in range(49, 65, 4):
                    t = (s - 49) // 4
                    e.wait_ge(S["vnew_ready"], SUB * n + t + 1)
                    if t == 0:
                        e.wait_ge(S["kd_ready"], n + 1)
                        e.wait_ge(S["ro_steps"], 6 * n + 6)
                    e.matmul(sub(bD_, t), sub(knat, t), rv_[:, 1, :], start=True, stop=True).then_inc(S["upd_out"], 1)
                    e.matmul(sub(bA, t), sub(attn, t), rv_[:, 1, :], start=True, stop=True).then_inc(S["o2_out"], 1)
            def out_step(b, last, j, k):
                step(out_quarter(b, last) + j // 4, j % 4, k // 4, k % 4, mT[:, :, k, :], acc[:, j % 2, :],
                     k == 0, k == KT - 1)

            def turned_out(n):
                e.wait_ge(S["go_steps"], 6 * n + 6)
                turn(bE, og).then_inc(S["go_t"], 1)

            def next_norm(b, n, s):
                if s == 40:
                    e.wait_ge(S["mix_r"], 3 * n + 1)
                    column_sums(norm_no(b, 0), bC)
                if s == 43:
                    row_everywhere(norm_no(b, 0), bC)

            def lead(q, pt):
                for s in range(LEAD):
                    project(q, pt, s)

            def unit(b, u, n, q, pt, first=LEAD, hn=None, norm=False):
                for s in range(first, UNIT * KT):
                    if q is not None:
                        project(q, pt, s, hn)
                    if s >= LEAD:
                        mix(b, u, n, s)
                    if norm:
                        next_norm(b, n, s)

            e.wait_ge(S["const_in"], 32)
            def mod_columns(g, bank):
                e.wait_ge(S["ada_sums"], KT * (g + 1))
                for j in range(16):
                    m = e.matmul(bank[:, 2 * (16 * g + j):2 * (16 * g + j) + 2], ada_acc[g][:, j * P:(j + 1) * P],
                                 ones[:, 0:2], start=True, stop=True)
                m.then_inc(S["mod_cols"], 1)

            mod_columns(0, bC)
            stats(0)
            e.wait_ge(S["wg_split"], 2)
            gate_rows(0)
            gate_columns(0)
            for s in range(UNIT * KT):
                i, k = s // KT, s % KT
                if k == 0 and i >= 2:
                    e.wait_ge(S["proj_evac"], i - 1)
                step(i // 4, i % 4, k // 4, k % 4, hT[:, :, k, :], acc[:, i % 2, :], k == 0, k == KT - 1)
            mod_columns(1, bC)
            mod_columns(2, bC)
            e.wait_ge(S["mod_ready"], 2)
            e.wait_ge(S["par_in"], 16)
            e.wait_ge(S["const_in"], 32)
            e.wait_ge(S["lmask_in"], 16)

            lead(quarter_of(0, 0), proj_of(0, 0))
            def block_of_tokens(b, last):
                with e.Fori(0, HEADS - 2) as u:
                    unit(b, u, b * HEADS + u, quarter_of(b, 0) + u * (UNIT // 4), proj_of(b, u))
                    lead(quarter_of(b, 0) + (u + 1) * (UNIT // 4), proj_of(b, u + 1))
                    turned_out(b * HEADS + u)
                n, q = b * HEADS + HEADS - 1, quarter_of(b, (HEADS - 1) * UNIT)
                unit(b, HEADS - 2, n - 1, quarter_of(b, (HEADS - 2) * UNIT), proj_of(b, HEADS - 2), norm=not last)
                turned_out(n - 1)
                if last:
                    unit(b, HEADS - 1, n, None, None)
                else:
                    e.wait_ge(S["row_kept"], 2 * b + 1)
                    unit(b, HEADS - 1, n, q, proj_of(b, HEADS - 1), first=0, hn=1 + 2 * b)

                e.wait_ge(S["mix_r"], 3 * HEADS * (b + 1))
                e.wait_ge(S["mix_g"], 3 * (HEADS * (b + 1) - 1))
                e.wait_ge(S["proj_evac"], proj_end(b, last) - 1)
                for k in range(KT - 1):
                    out_step(b, last, 0, k)
                turned_out(n)
                if not last:
                    gate_rows(1 + 2 * b)
                e.wait_ge(S["mix_g"], 3 * HEADS * (b + 1))
                out_step(b, last, 0, KT - 1)
                if not last:
                    gate_columns(b + 1)
                e.wait_ge(S["proj_evac"], proj_end(b, last))
                for j in range(1, KT):
                    if j >= 2:
                        e.wait_ge(S["out_evac"], KT * b + j - 1)
                    for k in range(KT):
                        out_step(b, last, j, k)
                stats(norm_no(b, 1) - last)

                def ff1(q, g, par, after):
                    for i in range(FFG):
                        if i >= 2 or after == "ff1":
                            e.wait_ge(S["ff1_evac"], NG * FFG * b + FFG * g + i - 1)
                        elif after == "ff2":
                            e.wait_ge(S["ff2_evac"], 2 * NG * FFG * b + 2 * FFG * (g - 1) - 1 + i)
                        else:
                            e.wait_ge(S["out_evac"], KT * (b + 1))
                        for k in range(KT):
                            if after == "out" and i == 0:
                                e.wait_ge(S["h_lo"], KT * (2 + 2 * b - last) + k + 1)
                            step(q, i, k // 4, k % 4, mT[:, :, k, :], acc[:, i % 2, :], k == 0, k == KT - 1)

                def ff2(q, g, par, after):
                    e.wait_ge(S["hid_lo"], NG * FFG * b + FFG * (g + 1))
                    for o in range(2 * FFG):
                        if o >= 2 or after == "ff2":
                            e.wait_ge(S["ff2_evac"], 2 * NG * FFG * b + 2 * FFG * g + o - 1)
                        else:
                            e.wait_ge(S["ff1_evac"], NG * FFG * b + FFG * (g + 2) - 1 + o)
                        for k in range(FFG):
                            step(q, o // 2, o % 2, k, hid[:, par, :, k, :], acc[:, o % 2, :], k == 0, k == FFG - 1)

                ffq = out_quarter(b, last) + KT // 4
                ff1(ffq, 0, 0, "out")
                ff1(ffq + 1, 1, 1, "ff1")
                ff2(ffq + 2, 0, 0, "ff1")
                with e.Fori(0, ff_pairs) as r:
                    ff1(ffq + 3 + 4 * r, 2 * r + 2, 0, "ff2")
                    ff2(ffq + 4 + 4 * r, 2 * r + 1, 1, "ff1")
                    ff1(ffq + 5 + 4 * r, 2 * r + 3, 1, "ff2")
                    ff2(ffq + 6 + 4 * r, 2 * r + 2, 0, "ff1")
                ff2(ffq + 2 * NG - 1, NG - 1, 1, "ff2")
                if not last:
                    e.wait_ge(S["ff2_evac"], 2 * NG * FFG * (b + 1) - 1)
                    lead(quarter_of(b + 1, 0), proj_of(b + 1, 0))
                stats(norm_no(b, 2) - last)

            with e.Fori(0, NB - 1) as b:
                block_of_tokens(b, False)
            block_of_tokens(NB - 1, True)

        @block.scalar
        def _(e):
            def hi(q, local):
                tile = local // 2
                e.wait_ge(RAWSEM[tile % NRAW], 16 * (2 * q + tile // NRAW + 1))
                if not isinstance(q, int) or 8 * q + local >= HALVES:
                    e.wait_ge(S["w_used"], 8 * q + local - HALVES + 1)
                e.activation(w2[:, 0, local % HALVES, :], raw[:, tile % NRAW, local % 2 * NT:(local % 2 + 1) * NT],
                             ACT.Copy).then_inc(S["w_hi"], 1)

            def io_written(b):
                for q in OSEM:
                    e.wait_ge(q, 32 * b)

            def square(n, j):
                if j >= 3:
                    e.wait_ge(S["sq_added"], (KT - 1) * n + j - 2)
                dst = sqrow if j == 0 else io[:, j % 2, :]
                e.activation(dst, x1[:, j, :], ACT.Square).then_inc(S["sq_ready"], 1)

            def modulated(hn, dst, A, B, used, count, tiles=range(KT)):
                e.wait_ge(used, count)
                for j in tiles:
                    e.wait_ge(S["xn_ready"], KT * hn + j + 1)
                    if j >= 2:
                        e.wait_ge(S["h_lo"], KT * hn + j - 1)
                    e.activation(io[:, 2 + j % 2, :], io[:, j % 2, :], ACT.Identity, scale=A[:, j:j + 1],
                                 bias=B[:, j:j + 1]).then_inc(S["hf_ready"], 1)
                    e.wait_ge(S["hf_ready"], KT * hn + j + 1)
                    e.activation(dst[:, 0, j, :], io[:, 2 + j % 2, :], ACT.Copy).then_inc(S["h_hi"], 1)

            def next_h(b, tiles, halves_left):
                modulated(1 + 2 * b, hT, A1, B1, S["w_used"], 8 * quarter_of(b, (HEADS - 1) * UNIT) - halves_left, tiles)

            def gate_exps(m):
                e.wait_ge(S["gate_steps"], GSTEPS * m + 3)
                e.activation(gu, gu, ACT.Exp, scale=-1.0).then_inc(S["gate_exp"], 1)
                e.activation(gbt, gbt, ACT.Exp, scale=-1.0).then_inc(S["gate_exp"], 1)

            def evac(n, q, i):
                e.wait_ge(S["w_used"], 8 * q + 2 * i + 2)
                if n is not None:
                    if i < 3:
                        e.wait_ge(S["conv_steps"], 12 * n + 12)
                    elif i == RK or i == RQ:
                        e.wait_ge(S["rot_cos_k"] if i == RK else S["rot_cos_q"], n + 1)
                        e.wait_ge(S["swap_k"] if i == RK else S["swap_q"], 2 * n + 2)
                    elif i == RV:
                        e.wait_ge(S["rt_out"], n + 1)
                    else:
                        e.wait_ge(S["y_rg"] if i == RG else S["y_gz"], n + 1)
                dst = pg[:, i, HIST:HIST + NT] if i < 3 else pr[:, i - 3, :]
                e.activation(dst, acc[:, i % 2, :], ACT.Copy).then_inc(S["proj_evac"], 1)

            def front(m, pt, s):
                if s == 41:
                    e.wait_ge(S["proj_evac"], pt - UNIT + RK + 1)
                    e.wait_ge(S["rot_q"], m)
                    e.activation(swp[0:64, :], pr[64:128, 0, :], ACT.Copy).then_inc(S["swap_k"], 1)
                    e.activation(swp[64:128, :], pr[0:64, 0, :], ACT.Copy).then_inc(S["swap_k"], 1)
                if s == 44:
                    e.wait_ge(S["conv_steps"], 12 * m + 4)
                    e.activation(tanh_at[GV], conv_at[GV], ACT.Tanh, scale=0.5).then_inc(S["tanh_v"], 1)
                if s == 47:
                    e.wait_ge(S["proj_evac"], pt - UNIT + RQ + 1)
                    e.wait_ge(S["rot_k"], m + 1)
                    e.activation(swp[0:64, :], pr[64:128, 1, :], ACT.Copy).then_inc(S["swap_q"], 1)
                    e.activation(swp[64:128, :], pr[0:64, 1, :], ACT.Copy).then_inc(S["swap_q"], 1)
                if s == 48:
                    e.wait_ge(S["conv_steps"], 12 * m + 8)
                    e.wait_ge(S["y_out"], (LEVELS - 1) * m)
                    e.activation(tanh_at[GQ], conv_at[GQ], ACT.Tanh, scale=0.5).then_inc(S["tanh_q"], 1)
                if s == 53:
                    e.wait_ge(S["conv_steps"], 12 * m + 12)
                    e.activation(tanh_at[GK], conv_at[GK], ACT.Tanh, scale=0.5).then_inc(S["tanh_k"], 1)

            def fronts(m, pt):
                for s in range(UNIT * KT):
                    front(m, pt, s)

            def unit(b, n, q, pt, next_front=True, norm=False):
                for s in range(UNIT * KT):
                    if s % 4 == 0 and q is not None:
                        hi(q, s // 4 + 3)
                    if s % 8 == 0 and s and q is not None:
                        evac(n, q, s // 8 - 1)
                    if s == 8:
                        e.wait_ge(S["d_out"], n + 1)
                        e.activation(Dm, bA, ACT.Exp).then_inc(S["d_exp"], 1)
                        e.wait_ge(S["gc_out"], n + 1)
                        e.activation(eg, bB[:, 0:12], ACT.Exp).then_inc(S["gc_exp"], 1)
                    if s == 9:
                        e.wait_ge(S["rt_out"], n + 1)
                        e.wait_ge(S["unit_start"], 4 * n + 4)
                        e.activation(rs[:, 0, :], bC, ACT.Copy, scale=cur[:, C_KDEC:C_KDEC + 1]).then_inc(S["kdec_r"], 1)
                        e.activation(rs[:, 1, :], bD_, ACT.Copy).then_inc(S["v_r"], 1)
                    if s == 12:
                        e.wait_ge(S["gt_out"], n + 1)
                        e.activation(sqk, bE, ACT.Square).then_inc(S["sqk_ready"], 1)
                        e.activation(sqq, bF, ACT.Square).then_inc(S["sqq_ready"], 1)
                        e.activation(vnat, bB, ACT.Copy, scale=0.5).then_inc(S["v_nat"], 1)
                    if s == 14:
                        e.activation(gts[:, 0, :], pr[:, RG - RK, :], ACT.Tanh, scale=0.5).then_inc(S["tanh_rg"], 1)
                        e.activation(gts[:, 1, :], pr[:, GZ - RK, :], ACT.Tanh, scale=0.5).then_inc(S["tanh_gz"], 1)
                    if s == 15:
                        e.wait_ge(S["kt_out"], n + 1)
                        e.activation(kT, bE, ACT.Copy).then_inc(S["kt_ready"], 1)
                    if s == 20:
                        e.wait_ge(S["t_first_out"], n + 1)
                        e.activation(T, bE, ACT.Copy).then_inc(S["t_ready"], 1)
                    if 22 <= s <= 42 and s % 4 == 2:
                        l = (s - 22) // 4 + 1
                        if l > 1:
                            e.wait_ge(S["y_out"], (LEVELS - 1) * n + l - 1)
                            e.wait_ge(S["t_turned"], (LEVELS - 2) * n + l - 1)
                            e.activation(U, bF, ACT.Copy).then_inc(S["u_turned"], 1)
                        e.wait_ge(S["x_out"], (LEVELS - 1) * n + l)
                        e.activation(X, bE, ACT.Copy).then_inc(S["x_ready"], 1)
                    if s == 31:
                        e.wait_ge(S["ro_steps"], 6 * n + 4)
                        e.activation(th, orr, ACT.Square).then_inc(S["rsq"], 1)
                    if s in range(47, 63, 4):
                        t = (s - 47) // 4
                        e.wait_ge(S["tr_out"], SUB * n + t + 1)
                        if t:
                            e.wait_ge(S["o2_out"], SUB * n + t)
                        e.activation(rv_[:, 1, :], sub(bE, t), ACT.Copy,
                                     scale=cgb[:, SUB + t:SUB + t + 1]).then_inc(S["vnew_ready"], 1)
                    if next_front:
                        front(n + 1, pt + UNIT, s)
                    if norm and 10 <= s < 10 + 3 * KT and (s - 10) % 3 == 0:
                        if s == 10:
                            e.wait_ge(S["x1_in"], 32 + 32 * b)
                            io_written(b)
                        square(norm_no(b, 0), (s - 10) // 3)
                    if norm and s == 61:
                        next_h(b, (0, 1), 1)
                if q is not None:
                    evac(n, q, UNIT - 1)
                e.wait_ge(S["go_steps"], 6 * n + 2)
                e.activation(Dm, og, ACT.Square).then_inc(S["gsq"], 1)

            e.wait_ge(S["mod_par_in"], 64)
            e.activation(scol, ccol, ACT.Exp, scale=-1.0).then_inc(S["silu_c"], 1)
            e.activation(negA, gpar[:, 0:4], ACT.Exp).then_inc(S["silu_c"], 1)
            e.wait_ge(S["const_in"], 32)
            e.activation(wgs[:, 0, :, :], wg[:, :, :], ACT.Copy).then_inc(S["wg_split"], 1)
            for h in range(3):
                hi(0, h)
            e.wait_ge(S["x1_in"], 16)
            e.wait_ge(S["mod_cols"], 1)
            for j in range(KT):
                square(0, j)
            modulated(0, hT, A1, B1, S["mod_ready"], 1)
            for i in range(UNIT):
                hi(0, 2 * i + 3)
                hi(0, 2 * i + 4)
                evac(None, 0, i)
                if i == 0:
                    gate_exps(0)

            e.wait_ge(S["mod_cols"], 3)
            fronts(0, proj_of(0, 0))

            def block_of_tokens(b, last):
                e.wait_ge(S["o_ready"], KT * b)
                e.dma_start(x1[:, :, :], xT[b if last else b + 1]).then_inc(S["x1_in"], 16)
                with e.Fori(0, HEADS - 2) as u:
                    unit(b, b * HEADS + u, quarter_of(b, 0) + u * (UNIT // 4), proj_of(b, u))
                n, q = b * HEADS + HEADS - 1, quarter_of(b, (HEADS - 1) * UNIT)
                unit(b, n - 1, quarter_of(b, (HEADS - 2) * UNIT), proj_of(b, HEADS - 2), norm=not last)
                if last:
                    io_written(b)
                    unit(b, n, None, None, next_front=False)
                else:
                    next_h(b, range(2, KT), 0)
                    e.wait_ge(S["xn_ready"], KT * (2 + 2 * b))
                    e.dma_start(x1[:, :, :], xT[b]).then_inc(S["x1_in"], 16)
                    unit(b, n, q, proj_of(b, HEADS - 1), next_front=False)
                    gate_exps(b + 1)
                    e.wait_ge(S["rot_q"], HEADS * (b + 1))
                    e.dma_start(cs[:, 0, :], cos[b + 1]).then_inc(S["cs_in"], 16)
                    e.dma_start(cs[:, 1, :], sin[b + 1]).then_inc(S["cs_in"], 16)
                for j in range(KT):
                    hi(out_quarter(b, last), 2 * j + 3)
                    if j:
                        e.wait_ge(S["out_evac"], KT * b + j)
                        square(norm_no(b, 1) - last, j - 1)
                    hi(out_quarter(b, last), 2 * j + 4)
                e.wait_ge(S["out_evac"], KT * (b + 1))
                square(norm_no(b, 1) - last, KT - 1)
                modulated(2 + 2 * b - last, mT, A2, B2, S["w_used"], 8 * (out_quarter(b, last) + KT // 4))

                def ff1(q, g, par):
                    for i in range(FFG):
                        f = NG * FFG * b + FFG * g + i
                        hi(q, 2 * i + 3)
                        hi(q, 2 * i + 4)
                        e.wait_ge(S["w_used"], 8 * q + 2 * i + 2)
                        if i >= 2:
                            e.wait_ge(S["ff1_evac"], f - 1)
                        e.activation(io[:, i % 2, :], acc[:, i % 2, :], ACT.Relu).then_inc(S["ff1_relu"], 1)
                        if i == 0:
                            e.wait_ge(S["w_used"], 8 * q)
                        e.wait_ge(S["ff1_evac"], f + 1)
                        e.activation(hid[:, par, 0, i, :], io[:, 2 + i % 2, :], ACT.Copy).then_inc(S["hid_hi"], 1)

                def ff2(q):
                    for i in range(FFG):
                        hi(q, 2 * i + 3)
                        hi(q, 2 * i + 4)

                ffq = out_quarter(b, last) + KT // 4
                ff1(ffq, 0, 0)
                ff1(ffq + 1, 1, 1)
                ff2(ffq + 2)
                with e.Fori(0, ff_pairs) as r:
                    ff1(ffq + 3 + 4 * r, 2 * r + 2, 0)
                    ff2(ffq + 4 + 4 * r)
                    ff1(ffq + 5 + 4 * r, 2 * r + 3, 1)
                    ff2(ffq + 6 + 4 * r)
                e.wait_ge(S["w_used"], 8 * (ffq + 2 * NG - 1))
                for o in range(KT):
                    hi(ffq + 2 * NG - 1, o + 3)
                    if o:
                        e.wait_ge(S["ff2_evac"], 2 * NG * FFG * (b + 1) - KT + o)
                        square(norm_no(b, 2) - last, o - 1)
                    if not last:
                        for s in range(36 + 3 * o, 39 + 3 * o):
                            front((b + 1) * HEADS, proj_of(b + 1, 0), s)
                e.wait_ge(S["ff2_evac"], 2 * NG * FFG * (b + 1))
                square(norm_no(b, 2) - last, KT - 1)
                for j in range(KT):
                    e.wait_ge(S["o_ready"], KT * b + j + 1)
                    e.dma_start(out[b, :, j, :], io[:, j % 4, :]).then_inc(OSEM[j % 4], 16)

            with e.Fori(0, NB - 1) as b:
                block_of_tokens(b, False)
            block_of_tokens(NB - 1, True)
            for q in OSEM:
                e.wait_ge(q, 32 * NB)

        @block.vector
        def _(e):
            one = 1.0

            def scaled_sums(n, bank):
                e.wait_ge(S["colsum_ready"], n + 1)
                e.tensor_scalar(ms, bank[:, 0:2 * SUB:2], 1.0 / D, EPS, ALU.mult, ALU.add).then_inc(S["ms_ready"], 1)

            def diagonal(n):
                e.wait_ge(S["rstd_ready"], n + 1)
                e.tensor_tensor(by_sub(dg), over_subs(ident), over_tokens(rstd), ALU.mult).then_inc(S["diag_ready"], 1)

            def row_of(n):
                scaled_sums(n, bB)
                diagonal(n)
                e.wait_ge(S["row_ready"], n + 1)

            def add_square(n, j):
                e.wait_ge(S["sq_ready"], KT * n + j + 1)
                if j > 1:
                    e.wait_ge(S["sq_added"], (KT - 1) * n + j - 1)
                e.tensor_tensor(sqrow, sqrow, io[:, j % 2, :], ALU.add).then_inc(S["sq_added"], 1)

            def normed(n, hn, row, tiles=range(KT)):
                e.wait_ge(S["sq_added"], (KT - 1) * (n + 1))
                for j in tiles:
                    if j >= 2:
                        e.wait_ge(S["hf_ready"], KT * hn + j - 1)
                    e.tensor_tensor(io[:, j % 2, :], x1[:, j, :], row, ALU.mult).then_inc(S["xn_ready"], 1)

            def gates(m):
                e.wait_ge(S["gate_rows"], m + 1)
                e.tensor_scalar(gateT[0:8, :], bF[0:8, :], one, None, ALU.mult).then_inc(S["gate_copied"], 1)
                done = [0]

                def go(ins):
                    ins.then_inc(S["gate_steps"], 1)
                    done[0] += 1

                def after(k=None):
                    e.wait_ge(S["gate_steps"], GSTEPS * m + (done[0] if k is None else k))

                def ht(x16):
                    return x16.rearrange("p (h t) -> p h t", t=SUB)

                raw8 = bF.rearrange("p (t c) -> p c t", c=P)[:, 0:8, :]
                e.wait_ge(S["gate_out"], m + 1)
                go(e.tensor_tensor(ht(gx), raw8[:, 0:4, :], gpar[:, 4:8].unsqueeze(2).to_broadcast([P, 4, SUB]), ALU.add))
                go(e.tensor_copy(ht(gbt), raw8[:, 4:8, :]))
                after(1)
                go(e.scalar_tensor_tensor(out=gu, in0=gx, scalar=-1.0, in1=gx, op0=ALU.mult, op1=ALU.max))
                e.wait_ge(S["gate_exp"], 2 * m + 2)
                go(e.tensor_scalar(gbt, gbt, one, None, ALU.add))
                after()
                go(e.reciprocal(gb[:, :, SUB:2 * SUB], ht(gbt)))
                go(e.tensor_scalar(gz_, gu, 2.0, None, ALU.add))
                after()
                go(e.reciprocal(gz_, gz_))
                after()
                go(e.tensor_tensor(gz_, gz_, gu, ALU.mult))
                after()
                go(e.tensor_tensor(gp, gz_, gz_, ALU.mult))
                after()
                go(e.tensor_scalar(gq_, gp, 1.0 / 15, None, ALU.mult))
                for c in (13, 11, 9, 7, 5, 3):
                    after()
                    go(e.scalar_tensor_tensor(out=gq_, in0=gq_, scalar=1.0 / c, in1=gp, op0=ALU.add, op1=ALU.mult))
                after()
                go(e.scalar_tensor_tensor(out=gq_, in0=gq_, scalar=one, in1=gz_, op0=ALU.add, op1=ALU.mult))
                after()
                go(e.tensor_scalar(gq_, gq_, 2.0, None, ALU.mult))
                after()
                go(e.scalar_tensor_tensor(out=gq_, in0=gx, scalar=0.0, in1=gq_, op0=ALU.max, op1=ALU.add))
                assert done[0] == GSTEPS
                after()
                e.tensor_tensor(gb[:, :, 0:SUB], ht(gq_), negA.unsqueeze(2).to_broadcast([P, 4, SUB]),
                                ALU.mult).then_inc(S["gates_done"], 1)

            def start_early(b, u, n):
                e.wait_ge(S["gates_done"], b + 1)
                e.wait_ge(S["state_kept"], 2 * n)
                e.tensor_scalar(cgb[:, :], gb[:, u, :], one, None, ALU.mult).then_inc(S["unit_start"], 1)
                e.tensor_scalar(Sr[:, :], states[:, 0, u, :], one, None, ALU.mult).then_inc(S["unit_start"], 1)
                e.tensor_scalar(Sg[:, :], states[:, 1, u, :], one, None, ALU.mult).then_inc(S["unit_start"], 1)
                twice_silu(S["tanh_q"], n, yq, tanh_at[GQ], conv_at[GQ], S["y_q"])

            def start_late(u, n):
                e.wait_ge(S["mix_g"], 3 * n)
                e.tensor_scalar(cur[:, :], para[:, u, :], one, None, ALU.mult).then_inc(S["unit_start"], 1)
                twice_silu(S["tanh_v"], n, yv, tanh_at[GV], conv_at[GV], S["y_v"])
                e.wait_ge(S["unit_start"], 4 * n + 4)

            def conv(m, order, i, taps):
                y = conv_at[i]
                for j in taps:
                    if j == 0:
                        e.tensor_scalar(y, pg[:, i, 0:NT], cw[:, TAPS * i:TAPS * i + 1], None,
                                        ALU.mult).then_inc(S["conv_steps"], 1)
                    else:
                        e.wait_ge(S["conv_steps"], 12 * m + TAPS * order + j)
                        e.scalar_tensor_tensor(out=y, in0=pg[:, i, j:j + NT], scalar=cw[:, TAPS * i + j:TAPS * i + j + 1],
                                               in1=y, op0=ALU.mult, op1=ALU.add).then_inc(S["conv_steps"], 1)

            def front(b, u, m, pt, s):
                if s == 39:
                    e.wait_ge(S["proj_evac"], pt - UNIT + 3)
                    e.wait_ge(S["conv_steps"], 12 * m)
                    e.tensor_scalar(cw[:, :], para[:, u, 0:3 * TAPS], one, None, ALU.mult).then_inc(S["front_start"], 1)
                    h3 = hist[:, u, :].rearrange("p (a c) -> p a c", a=3)
                    e.tensor_scalar(pg[:, :, 0:HIST], h3, one, None, ALU.mult).then_inc(S["front_start"], 1)
                    e.wait_ge(S["front_start"], 3 * m + 2)
                    e.tensor_scalar(h3, pg[:, :, NT:NT + HIST], one, None, ALU.mult).then_inc(S["front_start"], 1)
                    e.wait_ge(S["front_start"], 3 * m + 3)
                    conv(m, 0, GV, (0, 1))
                if s == 41:
                    conv(m, 0, GV, (2, 3))
                if s == 42:
                    e.wait_ge(S["lvl_mask"], (LEVELS - 1) * m)
                    conv(m, 1, GQ, (0, 1))
                if s == 43:
                    conv(m, 1, GQ, (2, 3))
                    e.wait_ge(S["cs_in"], 32 + 32 * b)
                if s == 45:
                    rotate(m, 0, S["swap_k"], S["rot_sin_k"], S["rot_cos_k"], S["rot_k"])
                if s == 47:
                    e.wait_ge(S["x_out"], (LEVELS - 1) * m)
                    conv(m, 2, GK, (0, 1))
                if s == 51:
                    conv(m, 2, GK, (2, 3))
                if s == 52:
                    rotate(m, 1, S["swap_q"], S["rot_sin_q"], S["rot_cos_q"], S["rot_q"])
                if s == 55:
                    twice_silu(S["tanh_k"], m, yk, tanh_at[GK], conv_at[GK], S["y_k"])

            def fronts(b, u, m, pt):
                for s in range(UNIT * KT):
                    front(b, u, m, pt, s)

            def twice_silu(tanh, n, y, t, x, done):
                e.wait_ge(tanh, n + 1)
                e.scalar_tensor_tensor(out=y, in0=t, scalar=one, in1=x, op0=ALU.add, op1=ALU.mult).then_inc(done, 1)

            def rotate(n, i, swap, sin_, cos_, done):
                e.wait_ge(swap, 2 * n + 2)
                e.tensor_tensor(swp, swp, cs[:, 1, :], ALU.mult).then_inc(sin_, 1)
                e.wait_ge(sin_, n + 1)
                e.wait_ge(cos_, n + 1)
                e.tensor_tensor(rot[:, i, :], rot[:, i, :], swp, ALU.add).then_inc(done, 1)

            def mixed(n, sem, bank, w, gate, y, dst):
                e.scalar_tensor_tensor(out=y, in0=bank, scalar=w, in1=gate, op0=ALU.mult, op1=ALU.mult).then_inc(sem, 1)
                e.wait_ge(sem, 3 * n + 1)
                e.tensor_scalar(dst(0), y, one, None, ALU.mult).then_inc(sem, 1)
                e.wait_ge(sem, 3 * n + 2)
                e.tensor_tensor(dst(1), y, dst(0).bitcast(F32), ALU.subtract).then_inc(sem, 1)

            def next_norm(b, s):
                n = norm_no(b, 0)
                if s >= 15 and s % 3 == 0 and s < 15 + 3 * (KT - 1):
                    add_square(n, (s - 12) // 3)
                if s == 40:
                    scaled_sums(n, bC)
                if s == 42:
                    diagonal(n)
                if s == 44:
                    e.wait_ge(S["row_ready"], n + 1)
                    e.tensor_copy(row1[:, :], bC).then_inc(S["row_kept"], 1)
                if s == 59:
                    e.wait_ge(S["row_kept"], 2 * b + 1)
                    normed(n, 1 + 2 * b, row1[:, :], (0, 1))

            def unit(b, u, n, pt=None, norm=False):
                for s in range(UNIT * KT):
                    if s == 8:
                        e.wait_ge(S["gc_exp"], n + 1)
                        e.tensor_scalar(negc, eg[:, 0:4], -1.0, None, ALU.mult).then_inc(S["negc_ready"], 1)
                    if s == 12:
                        e.wait_ge(S["sqk_ready"], n + 1)
                        e.tensor_reduce(ssk, by_sub(sqk), AX.X, ALU.add).then_inc(S["ss_steps"], 1)
                        e.wait_ge(S["ss_steps"], 4 * n + 1)
                        e.tensor_scalar(ssk, ssk, 4 * EPS, None, ALU.add).then_inc(S["ss_steps"], 1)
                    if s == 13:
                        e.wait_ge(S["nk_ready"], n + 1)
                        e.tensor_tensor(by_sub(knat), by_sub(bE), over_tokens(nk), ALU.mult).then_inc(S["k_nat"], 1)
                        e.wait_ge(S["sqq_ready"], n + 1)
                        e.tensor_reduce(ssq, by_sub(sqq), AX.X, ALU.add).then_inc(S["ss_steps"], 1)
                        e.wait_ge(S["ss_steps"], 4 * n + 3)
                        e.tensor_scalar(ssq, ssq, 4 * EPS, None, ALU.add).then_inc(S["ss_steps"], 1)
                        e.wait_ge(S["s_out"], n + 1)
                        e.tensor_tensor(by_sub(rs[:, 2, :]), by_sub(bA), over_subs(cur[:, PAR_MASK:PAR]),
                                        ALU.mult).then_inc(S["s_masked"], 1)
                    if s == 14:
                        twice_silu(S["tanh_rg"], n, gts[:, 0, :], gts[:, 0, :], pr[:, RG - RK, :], S["y_rg"])
                        twice_silu(S["tanh_gz"], n, gts[:, 1, :], gts[:, 1, :], pr[:, GZ - RK, :], S["y_gz"])
                    if s == 17:
                        e.wait_ge(S["kk_out"], n + 1)
                        e.wait_ge(S["beta_d"], n + 1)
                        e.tensor_tensor(LT, bB, bD, ALU.mult).then_inc(S["lt_ready"], 1)
                        e.wait_ge(S["lt_ready"], n + 1)
                        e.tensor_tensor(by_sub(Lm), by_sub(LT), over_subs(lmask[:, 0, :]), ALU.mult).then_inc(S["first_mask"], 1)
                    if s in (16, 20, 24):
                        t = (s - 16) // 4
                        e.wait_ge(S["r_cross"], SUB * n + t + 1)
                        e.wait_ge(S["r_upd"], n + 1)
                        if t:
                            e.wait_ge(S["r_state"], 3 * n + t)
                        e.scalar_tensor_tensor(out=Sr[:, :], in0=Sr[:, :], scalar=cur[:, C_SDEC:C_SDEC + 1],
                                               in1=sub(bA, t), op0=ALU.mult, op1=ALU.add).then_inc(S["r_state"], 1)
                    if s == 18:
                        e.wait_ge(S["first_mask"], n + 1)
                        e.tensor_tensor(by_sub(U), over_subs(ident), by_sub(Lm), ALU.subtract).then_inc(S["u_first"], 1)
                        e.tensor_tensor(attn, bF, Dm, ALU.mult).then_inc(S["attn_ready"], 1)
                    if 24 <= s <= 44 and s % 4 == 0:
                        l = (s - 24) // 4 + 1
                        e.wait_ge(S["y_out"], (LEVELS - 1) * n + l)
                        if l < LEVELS - 1:
                            if l > 1:
                                e.wait_ge(S["t_next"], (LEVELS - 2) * n + l - 1)
                            else:
                                e.wait_ge(S["t_ready"], n + 1)
                            e.tensor_tensor(T, T, bB, ALU.subtract).then_inc(S["t_next"], 1)
                        else:
                            e.wait_ge(S["u_turned"], (LEVELS - 2) * (n + 1))
                            e.tensor_tensor(U, U, bF, ALU.subtract).then_inc(S["u_next"], 1)
                    if s == 28:
                        e.wait_ge(S["r_cross"], SUB * n + SUB)
                        e.wait_ge(S["r_state"], 3 * n + 3)
                        e.scalar_tensor_tensor(out=Sr[:, :], in0=Sr[:, :], scalar=cur[:, C_SDEC:C_SDEC + 1],
                                               in1=sub(bA, SUB - 1), op0=ALU.mult, op1=ALU.add).then_inc(S["state_kept"], 1)
                        e.tensor_scalar(orr, bC, cur[:, C_QDEC:C_QDEC + 1], None, ALU.mult).then_inc(S["ro_steps"], 1)
                        e.wait_ge(S["ro_steps"], 6 * n + 1)
                        e.tensor_tensor(orr, orr, bD_, ALU.add).then_inc(S["ro_steps"], 1)
                        e.wait_ge(S["ro_steps"], 6 * n + 2)
                        e.tensor_reduce(rme, by_sub(orr), AX.X, ALU.add).then_inc(S["ro_steps"], 1)
                        e.wait_ge(S["ro_steps"], 6 * n + 3)
                        e.scalar_tensor_tensor(out=by_sub(orr), in0=over_tokens(rme), scalar=-1.0 / P, in1=by_sub(orr),
                                               op0=ALU.mult, op1=ALU.add).then_inc(S["ro_steps"], 1)
                        e.wait_ge(S["state_kept"], 2 * n + 1)
                        e.tensor_scalar(states[:, 0, u, :], Sr[:, :], one, None, ALU.mult).then_inc(S["sr_kept"], 1)
                    if s == 32:
                        e.wait_ge(S["rsq"], n + 1)
                        e.tensor_reduce(rva, by_sub(th), AX.X, ALU.add).then_inc(S["rvar"], 1)
                        e.wait_ge(S["rvar"], n + 1)
                        e.tensor_scalar(rva, rva, 4.0 / P, 4 * EPS, ALU.mult, ALU.add).then_inc(S["ro_steps"], 1)
                    if s == 34:
                        e.wait_ge(S["rpow"], n + 1)
                        e.tensor_tensor(by_sub(orr), by_sub(orr), over_tokens(rrs), ALU.mult).then_inc(S["ro_steps"], 1)
                    if s == 37:
                        e.wait_ge(S["ro_t"], n + 1)
                        e.wait_ge(S["w_used"], 8 * quarter_of(b, 0))
                        mixed(n, S["mix_r"], bC, cur[:, C_RETW:C_RETW + 1], gts[:, 0, :], orr, lambda h: mT[:, h, u, :])
                    if s in range(46, 62, 4):
                        t = (s - 46) // 4
                        e.wait_ge(S["ks_out"], SUB * n + t + 1)
                        if t == 0:
                            e.wait_ge(S["negc_ready"], n + 1)
                        else:
                            e.wait_ge(S["tr_out"], SUB * n + t)
                        e.scalar_tensor_tensor(out=rv_[:, 0, :], in0=sub(bB, t), scalar=negc[:, t:t + 1],
                                               in1=sub(vnat, t), op0=ALU.mult, op1=ALU.add).then_inc(S["r_ready"], 1)
                    if s in range(49, 65, 4):
                        t = (s - 49) // 4
                        e.wait_ge(S["upd_out"], SUB * n + t + 1)
                        if t:
                            e.wait_ge(S["g_state"], SUB * n + t)
                        e.scalar_tensor_tensor(out=Sg[:, :], in0=Sg[:, :], scalar=eg[:, 8 + t:9 + t],
                                               in1=sub(bD_, t), op0=ALU.mult, op1=ALU.add).then_inc(S["g_state"], 1)
                    if pt is not None:
                        front(b, u + 1, n + 1, pt + UNIT, s)
                    if norm:
                        next_norm(b, s)
                e.wait_ge(S["o2_out"], SUB * n + SUB)
                e.tensor_tensor(by_sub(og), by_sub(bF), over_tokens(eg[:, 0:4]), ALU.mult).then_inc(S["go_steps"], 1)
                e.wait_ge(S["go_steps"], 6 * n + 1)
                e.tensor_tensor(og, og, bA, ALU.add).then_inc(S["go_steps"], 1)
                e.wait_ge(S["nq_ready"], n + 1)
                e.tensor_tensor(gtm, nq, nq, ALU.mult).then_inc(S["gfac"], 1)
                e.wait_ge(S["g_state"], SUB * n + SUB)
                e.tensor_scalar(states[:, 1, u, :], Sg[:, :], one, None, ALU.mult).then_inc(S["state_kept"], 1)
                e.wait_ge(S["gsq"], n + 1)
                e.tensor_reduce(gva, by_sub(Dm), AX.X, ALU.add).then_inc(S["go_steps"], 1)
                e.wait_ge(S["gfac"], n + 1)
                e.wait_ge(S["go_steps"], 6 * n + 3)
                e.tensor_tensor(gtm, gtm, gva, ALU.mult).then_inc(S["go_steps"], 1)
                e.wait_ge(S["go_steps"], 6 * n + 4)
                e.tensor_scalar(gtm, gtm, 4.0 / (P * DK), 4 * EPS, ALU.mult, ALU.add).then_inc(S["gvar"], 1)
                e.wait_ge(S["gpow"], n + 1)
                e.scalar_tensor_tensor(out=gfa, in0=nq, scalar=float(DK) ** -0.5, in1=grs, op0=ALU.mult,
                                       op1=ALU.mult).then_inc(S["go_steps"], 1)
                e.wait_ge(S["go_steps"], 6 * n + 5)
                e.tensor_tensor(by_sub(og), by_sub(og), over_tokens(gfa), ALU.mult).then_inc(S["go_steps"], 1)
                if pt is not None:
                    start_early(b, u + 1, n + 1)
                e.wait_ge(S["go_t"], n + 1)
                mixed(n, S["mix_g"], bE, cur[:, C_GDNW:C_GDNW + 1], gts[:, 1, :], og, lambda h: mT[:, h, HEADS + u, :])

            e.memset(mhalf, -0.5).then_inc(S["host_consts"], 1)
            e.memset(states[:, :, :, :], 0.0).then_inc(S["host_consts"], 1)
            e.memset(hist[:, :, :], 0.0).then_inc(S["host_consts"], 1)
            e.wait_ge(S["silu_c"], 2)
            e.wait_ge(S["mod_par_in"], 64)
            e.tensor_scalar(negA, negA, -1.0, None, ALU.mult).then_inc(S["silu_v"], 1)
            e.tensor_scalar(scol, scol, one, None, ALU.add).then_inc(S["silu_v"], 1)
            e.wait_ge(S["silu_v"], 2)
            e.reciprocal(scol, scol).then_inc(S["silu_v"], 1)
            e.wait_ge(S["silu_v"], 3)
            e.tensor_tensor(scol, scol, ccol, ALU.mult).then_inc(S["silu_v"], 1)
            e.wait_ge(S["silu_v"], 4)
            def ada_sum(g):
                for j in range(KT):
                    k = KT * g + j
                    e.wait_ge(ADASEM[ada_at[k]], 16 * (ada_turn[k] + 1))
                    if j == 0:
                        ins = e.tensor_scalar(ada_acc[g], ada_slot(k), scol[:, 0:1], None, ALU.mult)
                    else:
                        e.wait_ge(S["ada_sums"], k)
                        ins = e.scalar_tensor_tensor(out=ada_acc[g], in0=ada_slot(k), scalar=scol[:, j:j + 1],
                                                     in1=ada_acc[g], op0=ALU.mult, op1=ALU.add)
                    ins.then_inc(S["ada_sums"], 1)

            ada_sum(0)
            e.wait_ge(S["mod_cols"], 1)
            e.tensor_tensor(mod[:, 0:16], bC[:, 0:32:2], adab[:, 0:16], ALU.add).then_inc(S["mod_steps"], 1)
            e.wait_ge(S["mod_steps"], 1)
            e.tensor_copy(B1, mod[:, 0:8]).then_inc(S["mod_steps"], 1)
            e.scalar_tensor_tensor(out=A1, in0=mod[:, 8:16], scalar=one, in1=nrm[:, 0:8], op0=ALU.add,
                                   op1=ALU.mult).then_inc(S["mod_steps"], 1)
            e.wait_ge(S["mod_steps"], 3)
            e.wait_ge(S["host_consts"], 3)
            e.wait_ge(S["wg_split"], 1)
            e.tensor_tensor(wgs[:, 1, :, :], wg[:, :, :], wgs[:, 0, :, :].bitcast(F32), ALU.subtract).then_inc(S["wg_split"], 1)
            e.sem_inc(S["mod_ready"], 1)
            e.wait_ge(S["x1_in"], 16)
            for j in range(1, KT):
                add_square(0, j)
            row_of(0)
            normed(0, 0, bA)
            e.wait_ge(S["xn_ready"], KT)
            gates(0)
            ada_sum(1)
            ada_sum(2)
            e.wait_ge(S["mod_cols"], 3)
            e.tensor_tensor(mod[:, 16:48], bC[:, 32:96:2], adab[:, 16:48], ALU.add).then_inc(S["mod_steps"], 1)
            e.wait_ge(S["mod_steps"], 4)
            e.tensor_copy(GA, mod[:, 16:24]).then_inc(S["mod_steps"], 1)
            e.tensor_copy(B2, mod[:, 24:32]).then_inc(S["mod_steps"], 1)
            e.tensor_copy(GM, mod[:, 40:48]).then_inc(S["mod_steps"], 1)
            e.tensor_copy(WF, nrm[:, 16:24]).then_inc(S["mod_steps"], 1)
            e.scalar_tensor_tensor(out=A2, in0=mod[:, 32:40], scalar=one, in1=nrm[:, 8:16], op0=ALU.add,
                                   op1=ALU.mult).then_inc(S["mod_steps"], 1)
            e.wait_ge(S["mod_steps"], 9)
            e.sem_inc(S["mod_ready"], 1)

            fronts(0, 0, 0, proj_of(0, 0))
            e.wait_ge(S["lmask_in"], 16)
            start_early(0, 0, 0)
            start_late(0, 0)

            def block_of_tokens(b, last):
                with e.Fori(0, HEADS - 2) as u:
                    unit(b, u, b * HEADS + u, proj_of(b, u))
                    start_late(u + 1, b * HEADS + u + 1)
                n = b * HEADS + HEADS - 1
                unit(b, HEADS - 2, n - 1, proj_of(b, HEADS - 2), norm=not last)
                if not last:
                    normed(norm_no(b, 0), 1 + 2 * b, row1[:, :], range(2, KT))
                start_late(HEADS - 1, n)
                unit(b, HEADS - 1, n)
                if not last:
                    gates(b + 1)
                e.wait_ge(S["x1_in"], (32 if last else 48) + 32 * b)
                for j in range(KT):
                    e.wait_ge(S["w_used"], 8 * out_quarter(b, last) + 2 * j + 2)
                    e.scalar_tensor_tensor(out=x1[:, j, :], in0=acc[:, j % 2, :], scalar=GA[:, j:j + 1],
                                           in1=x1[:, j, :], op0=ALU.mult, op1=ALU.add).then_inc(S["out_evac"], 1)
                    if j >= 2:
                        add_square(norm_no(b, 1) - last, j - 1)
                add_square(norm_no(b, 1) - last, KT - 1)
                row_of(norm_no(b, 1) - last)
                normed(norm_no(b, 1) - last, 2 + 2 * b - last, bA)

                def ff1(g):
                    for i in range(FFG):
                        f = NG * FFG * b + FFG * g + i
                        e.wait_ge(S["ff1_relu"], f + 1)
                        e.wait_ge(S["hid_lo"], f - 1 if i >= 2 else NG * FFG * b + FFG * g)
                        e.scalar_tensor_tensor(out=io[:, 2 + i % 2, :], in0=acc[:, i % 2, :], scalar=0.0,
                                               in1=io[:, i % 2, :], op0=ALU.max, op1=ALU.mult).then_inc(S["ff1_evac"], 1)

                def ff2(q, g, squares=False):
                    for o in range(2 * FFG):
                        f = 2 * NG * FFG * b + 2 * FFG * g + o
                        e.wait_ge(S["w_used"], 8 * q + o + 1)
                        e.wait_ge(S["ff2_evac"], f)
                        e.scalar_tensor_tensor(out=x1[:, o, :], in0=acc[:, o % 2, :], scalar=GM[:, o:o + 1],
                                               in1=x1[:, o, :], op0=ALU.mult, op1=ALU.add).then_inc(S["ff2_evac"], 1)
                        if squares and o >= 2:
                            add_square(norm_no(b, 2) - last, o - 1)
                        if squares and not last:
                            for s in range(36 + 3 * o, 39 + 3 * o):
                                front(b + 1, 0, (b + 1) * HEADS, proj_of(b + 1, 0), s)

                ffq = out_quarter(b, last) + KT // 4
                ff1(0)
                ff1(1)
                ff2(ffq + 2, 0)
                with e.Fori(0, ff_pairs) as r:
                    ff1(2 * r + 2)
                    ff2(ffq + 4 + 4 * r, 2 * r + 1)
                    ff1(2 * r + 3)
                    ff2(ffq + 6 + 4 * r, 2 * r + 2)
                e.wait_ge(S["w_used"], 8 * (ffq + 2 * NG - 1))
                ff2(ffq + 2 * NG - 1, NG - 1, squares=True)
                add_square(norm_no(b, 2) - last, KT - 1)
                if not last:
                    start_early(b + 1, 0, (b + 1) * HEADS)
                    start_late(0, (b + 1) * HEADS)
                row_of(norm_no(b, 2) - last)
                e.tensor_copy(row1[:, :], bA).then_inc(S["row_kept"], 1)
                e.wait_ge(S["row_kept"], 2 * b + (1 if last else 2))
                for j in range(KT):
                    if j >= 4:
                        e.wait_ge(OSEM[j % 4], 16 * (2 * b + 1))
                    e.scalar_tensor_tensor(out=io[:, j % 4, :], in0=x1[:, j, :], scalar=WF[:, j:j + 1], in1=row1[:, :],
                                           op0=ALU.mult, op1=ALU.mult).then_inc(S["o_ready"], 1)

            with e.Fori(0, NB - 1) as b:
                block_of_tokens(b, False)
            block_of_tokens(NB - 1, True)

        @block.gpsimd
        def _(e):
            def lo(q, local):
                tile = local // 2
                e.wait_ge(S["w_hi"], 8 * q + local + 1)
                e.tensor_tensor(w2[:, 1, local % HALVES, :], raw[:, tile % NRAW, local % 2 * NT:(local % 2 + 1) * NT],
                                w2[:, 0, local % HALVES, :].bitcast(F32), ALU.subtract).then_inc(S["w_lo"], 1)

            def rms_power(n):
                e.wait_ge(S["ms_ready"], n + 1)
                e.tensor_tensor(rstd, ms, mhalf[:, 0:4], ALU.pow).then_inc(S["rstd_ready"], 1)

            def low_parts(hn, dst, tiles=range(KT)):
                for j in tiles:
                    e.wait_ge(S["h_hi"], KT * hn + j + 1)
                    e.tensor_tensor(dst[:, 1, j, :], io[:, 2 + j % 2, :], dst[:, 0, j, :].bitcast(F32),
                                    ALU.subtract).then_inc(S["h_lo"], 1)

            def front(b, u, m, pt, s):
                if s == 40:
                    e.wait_ge(S["r_cross"], SUB * m)
                    e.wait_ge(S["proj_evac"], pt - UNIT + RK + 1)
                    e.wait_ge(S["cs_in"], 32 + 32 * b)
                    e.tensor_tensor(rot[:, 0, :], pr[:, 0, :], cs[:, 0, :], ALU.mult).then_inc(S["rot_cos_k"], 1)
                if s == 42:
                    e.wait_ge(S["proj_evac"], pt - UNIT + RQ + 1)
                    e.tensor_tensor(rot[:, 1, :], pr[:, 1, :], cs[:, 0, :], ALU.mult).then_inc(S["rot_cos_q"], 1)
                if s == 45:
                    e.wait_ge(S["gates_done"], b + 1)
                    e.wait_ge(S["lt_ready"], m)
                    e.tensor_tensor(by_sub(gs), over_subs(strict), over_tokens(gb[:, u, 0:SUB]), ALU.mult).then_inc(S["gstrict"], 1)

            def fronts(b, u, m, pt):
                for s in range(UNIT * KT):
                    front(b, u, m, pt, s)

            def unit(b, n, q, u=None, pt=None, norm=False):
                for s in range(UNIT * KT):
                    if s % 4 == 0 and q is not None:
                        lo(q, s // 4 + 3)
                    if s == 41 and norm:
                        rms_power(norm_no(b, 0))
                    if s == 9:
                        e.wait_ge(S["d_exp"], n + 1)
                        e.tensor_tensor(by_sub(Dm), by_sub(Dm), over_subs(upper), ALU.mult).then_inc(S["d_mask"], 1)
                    if s == 11:
                        e.wait_ge(S["d_mask"], n + 1)
                        e.tensor_tensor(by_sub(bD), by_sub(Dm), over_tokens(cgb[:, SUB:2 * SUB]), ALU.mult).then_inc(S["beta_d"], 1)
                    if s == 12:
                        e.wait_ge(S["ss_steps"], 4 * n + 2)
                        e.tensor_tensor(nk, ssk, mhalf[:, 0:4], ALU.pow).then_inc(S["nk_ready"], 1)
                    if s == 14:
                        e.wait_ge(S["ss_steps"], 4 * n + 4)
                        e.tensor_tensor(nq, ssq, mhalf[:, 0:4], ALU.pow).then_inc(S["nq_ready"], 1)
                    if 18 <= s <= 38 and s % 4 == 2:
                        l = (s - 18) // 4 + 1
                        if l == 1:
                            e.wait_ge(S["u_first"], n + 1)
                        else:
                            e.wait_ge(S["x_out"], (LEVELS - 1) * n + l - 1)
                        e.tensor_tensor(by_sub(Lm), by_sub(LT), over_subs(lmask[:, l, :]), ALU.mult).then_inc(S["lvl_mask"], 1)
                    if s == 33:
                        e.wait_ge(S["ro_steps"], 6 * n + 5)
                        e.tensor_tensor(rrs, rva, mhalf[:, 0:4], ALU.pow).then_inc(S["rpow"], 1)
                    if s == 41:
                        e.wait_ge(S["kt_out"], n + 1)
                        e.wait_ge(S["gc_exp"], n + 1)
                        e.tensor_tensor(by_sub(knat), by_sub(knat), over_tokens(eg[:, 4:8]), ALU.mult).then_inc(S["kd_ready"], 1)
                    if pt is not None:
                        front(b, u, n + 1, pt + UNIT, s)
                if norm:
                    low_parts(1 + 2 * b, hT, (0, 1))
                e.wait_ge(S["gvar"], n + 1)
                e.tensor_tensor(grs, gtm, mhalf[:, 0:4], ALU.pow).then_inc(S["gpow"], 1)

            e.wait_ge(S["const_in"], 32)
            e.wait_ge(S["lmask_in"], 16)
            e.wait_ge(S["host_consts"], 3)
            for h in range(3):
                lo(0, h)
            rms_power(0)
            low_parts(0, hT)
            for i in range(UNIT):
                lo(0, 2 * i + 3)
                lo(0, 2 * i + 4)
            e.wait_ge(S["mod_ready"], 2)
            fronts(0, 0, 0, proj_of(0, 0))

            def block_of_tokens(b, last):
                with e.Fori(0, HEADS - 2) as u:
                    unit(b, b * HEADS + u, quarter_of(b, 0) + u * (UNIT // 4), u + 1, proj_of(b, u))
                n, q = b * HEADS + HEADS - 1, quarter_of(b, (HEADS - 1) * UNIT)
                unit(b, n - 1, quarter_of(b, (HEADS - 2) * UNIT), HEADS - 1, proj_of(b, HEADS - 2), norm=not last)
                if not last:
                    low_parts(1 + 2 * b, hT, range(2, KT))
                unit(b, n, None if last else q)
                for j in range(2 * KT):
                    lo(out_quarter(b, last), j + 3)
                rms_power(norm_no(b, 1) - last)
                low_parts(2 + 2 * b - last, mT)

                def ff1(q, g, par):
                    for i in range(FFG):
                        lo(q, 2 * i + 3)
                        lo(q, 2 * i + 4)
                        e.wait_ge(S["hid_hi"], NG * FFG * b + FFG * g + i + 1)
                        e.tensor_tensor(hid[:, par, 1, i, :], io[:, 2 + i % 2, :], hid[:, par, 0, i, :].bitcast(F32),
                                        ALU.subtract).then_inc(S["hid_lo"], 1)

                def ff2(q):
                    for i in range(2 * FFG):
                        lo(q, i + 3)

                ffq = out_quarter(b, last) + KT // 4
                ff1(ffq, 0, 0)
                ff1(ffq + 1, 1, 1)
                ff2(ffq + 2)
                with e.Fori(0, ff_pairs) as r:
                    ff1(ffq + 3 + 4 * r, 2 * r + 2, 0)
                    ff2(ffq + 4 + 4 * r)
                    ff1(ffq + 5 + 4 * r, 2 * r + 3, 1)
                    ff2(ffq + 6 + 4 * r)
                for o in range(2 * FFG):
                    lo(ffq + 2 * NG - 1, o + 3)
                    if not last:
                        if o == 0:
                            e.wait_ge(S["w_used"], 8 * (ffq + 2 * NG - 1))
                        for s in range(36 + 3 * o, 39 + 3 * o):
                            front(b + 1, 0, (b + 1) * HEADS, proj_of(b + 1, 0), s)
                rms_power(norm_no(b, 2) - last)

            with e.Fori(0, NB - 1) as b:
                block_of_tokens(b, False)
            block_of_tokens(NB - 1, True)


def constants():
    r = np.arange(P)
    f = np.float32
    masks = np.zeros((P, 4 + LEVELS, P), f)
    masks[:, 0] = np.eye(P)
    masks[:, 1] = 1.0
    masks[:, 2] = r[:, None] <= r[None, :]
    masks[:, 3] = r[:, None] > r[None, :]
    for l in range(LEVELS):
        m = 1 << l
        masks[:, 4 + l] = ((r[:, None] // (2 * m) == r[None, :] // (2 * m))
                           & (r[:, None] // m % 2 == 0) & (r[None, :] // m % 2 == 1))
    inv = (10000.0 ** (-np.arange(0, DK, 2, dtype=f) / f(DK))).astype(f)
    ang = (np.arange(SEQ, dtype=f)[:, None] * inv[None, :]).astype(f).astype(np.float64)
    cos, sin = np.cos(ang).T, np.sin(ang).T
    cos = np.concatenate([cos, cos]).astype(f).reshape(P, NB, NT).transpose(1, 0, 2)
    sin = np.concatenate([-sin, sin]).astype(f).reshape(P, NB, NT).transpose(1, 0, 2)
    par = np.zeros((P, HEADS, PAR), f)
    s, c = r[:, None], r[None, :]
    for h in range(HEADS):
        lg = np.log(1.0 - 2.0 ** (-5.0 - h))
        scale = DK ** -0.5
        par[:, h, C_QDEC] = np.exp(lg * (r + 1))
        par[:, h, C_KDEC] = np.exp(lg * (P - 1 - r)) * scale
        par[:, h, C_SDEC] = np.exp(lg * P)
        seen = (s // CHUNK) <= (c // CHUNK)
        par[:, h, PAR_MASK:] = np.where(seen, np.exp(lg * np.abs(c - s)), 0.0) * scale
    return masks, np.ascontiguousarray(cos), np.ascontiguousarray(sin), par


def layout(x, c, ada_w, ada_b, norm_mix_w, w_in, conv_w, a_log, dt_bias, ret_norm_w, gdn_norm_w, w_out,
           norm_mlp_w, w_ff1, w_ff2, norm_final_w):
    masks, cos, sin, par = constants()

    def cols(v):
        return v.reshape(-1, P).T

    def tile(w):
        return w.reshape(KT, P, P).transpose(1, 0, 2).reshape(P, KT * P)

    w_in, w_out, w1, w2 = w_in[0], w_out[0], w_ff1[0], w_ff2[0]
    first = {RQ: 0, RK: 512, RV: 1024, RG: 1536, GQ: 2048, GK: 2560, GV: 3072, GZ: 3584}
    stream = []
    for u in (1, 2, 3, 0):
        for i in range(UNIT):
            at = first[i] + u * P
            stream.append(tile(w_in[:, at:at + P]))
    for j in range(KT):
        stream.append(tile(w_out[:, j * P:(j + 1) * P]))

    def ff1(g):
        for i in range(FFG):
            at = (g * FFG + i) * P
            stream.append(tile(w1[:, at:at + P]))

    def ff2(g):
        rows = w2[g * FFG * P:(g + 1) * FFG * P].reshape(FFG, P, KT, P)
        for i in range(FFG):
            part = rows[:, :, 2 * i:2 * i + 2, :]
            stream.append(part.transpose(1, 2, 0, 3).reshape(P, KT * P))

    ff1(0)
    for g in range(1, NG):
        ff1(g)
        ff2(g - 1)
    ff2(NG - 1)
    assert len(stream) == TILES_PER_BLOCK

    conv = conv_w[0].reshape(TAPS, 3, HEADS, P)
    for h in range(HEADS):
        for slot, which in ((GK, 1), (GQ, 0), (GV, 2)):
            par[:, h, 4 * slot:4 * slot + 4] = conv[:, which, h, :].T
        par[:, h, C_RETW] = ret_norm_w[0, h * P:(h + 1) * P]
        par[:, h, C_GDNW] = gdn_norm_w[0]
    return {
        "xT": x[0].reshape(NB, NT, KT, P).transpose(0, 3, 2, 1),
        "w_all": np.stack(stream),
        "w_gate": w_in[:, 4096:4104].reshape(KT, P, 8).transpose(1, 0, 2),
        "ada_w": ada_w[0].reshape(KT, P, 3, 2048).transpose(2, 0, 1, 3),
        "c_col": cols(c[0]),
        "ada_b": cols(ada_b[0]),
        "norms": np.concatenate([cols(norm_mix_w[0]), cols(norm_mlp_w[0]), cols(norm_final_w)], axis=1),
        "par": par,
        "masks": masks,
        "cos": cos,
        "sin": sin,
        "gate_par": np.broadcast_to(np.concatenate([a_log[0], dt_bias[0]])[None, :], (P, 8)),
    }


def kernel(**inputs):
    import concourse.bacc as bacc
    from concourse.bass_utils import run_bass_kernel_spmd

    nc = bacc.Bacc("TRN2", target_bir_lowering=False, num_devices=1)
    laid = layout(**{k: np.asarray(v) for k, v in inputs.items()})
    arrays, args = {}, []
    for name, a in laid.items():
        a = np.ascontiguousarray(a)
        arrays[f"in_{name}"] = a
        args.append(nc.dram_tensor(f"in_{name}", a.shape, mybir.dt.from_np(a.dtype), kind="ExternalInput").ap())
    out = nc.dram_tensor("out_0", (NB, P, KT, NT), F32, kind="ExternalOutput").ap()
    build(nc, *args, out)
    r = run_bass_kernel_spmd(nc, [arrays], core_ids=[0])
    o = r.results[0]["out_0"]
    return np.ascontiguousarray(o.transpose(0, 3, 2, 1).reshape(1, SEQ, D))
```
